# Optimizing a Trainium2 kernel written in Bass

```python
import math
import jax, jax.numpy as jnp
from jax import lax
import numpy as np

D_MODEL = 1024
BATCH = 1
SEQ = 256
DEPTH = 2
DEC_BATCH = 8
DEC_SEQ = 4
PAST_LEN = 2048
PAGE_SIZE = 128

N_EVEN = (DEPTH + 1) // 2
N_ODD = DEPTH // 2

SSD_HEAD_DIM = 64
SSD_WIDTH = D_MODEL
SSD_HEADS = SSD_WIDTH // SSD_HEAD_DIM
SSD_GROUPS = 2
SSD_STATE = 128
SSD_CONV = 4
SSD_CHUNK = 128
CONV_DIM = SSD_WIDTH + 2 * SSD_GROUPS * SSD_STATE

ATT_HEAD_DIM = 64
ATT_HEADS = D_MODEL // ATT_HEAD_DIM
ATT_KV_HEADS = 4
ATT_REP = ATT_HEADS // ATT_KV_HEADS
WINDOW = 128
Q_DIM = ATT_HEADS * ATT_HEAD_DIM
KV_DIM = ATT_KV_HEADS * ATT_HEAD_DIM

IN_DIM = SSD_WIDTH + CONV_DIM + SSD_HEADS + Q_DIM + 2 * KV_DIM
MIX_DIM = SSD_WIDTH + Q_DIM

RWKV_HEAD = 64
RWKV_HEADS = D_MODEL // RWKV_HEAD
DECAY_LORA = 64
ICLR_LORA = 64
GATE_LORA = 128
RWKV_GN_EPS = 64e-5

D_FF = 2816
N_EXPERTS = 8
TOP_K = 2
EXPERT_FF = 2816

RMS_EPS = 1e-6
NEG_INF = -1e30

kernel_name = 'hybrid_ssd_swa_rwkv7_moe_step'

def _rms(x, w):
    xf = x.astype(jnp.float32)
    y = xf * lax.rsqrt(jnp.mean(xf * xf, axis=-1, keepdims=True) + RMS_EPS)
    return (y * w.astype(jnp.float32)).astype(x.dtype)

def _swiglu(h, wg, wu, wd):
    return (jax.nn.silu(h @ wg) * (h @ wu)) @ wd

def _causal_conv(xbc, buf, w, b):
    L = xbc.shape[1]
    full = jnp.concatenate([buf.astype(xbc.dtype), xbc], axis=1)
    out = b + sum(full[:, j:j + L] * w[j] for j in range(SSD_CONV))
    return jax.nn.silu(out), full[:, L:]

def _ssd_scan(x, dt, A, Bm, Cm, h0):
    b, L = x.shape[:2]
    q = min(SSD_CHUNK, L)
    pad = (-L) % q
    if pad:
        padfn = lambda t: jnp.pad(t, [(0, 0), (0, pad)] + [(0, 0)] * (t.ndim - 2))
        x, dt, Bm, Cm = padfn(x), padfn(dt), padfn(Bm), padfn(Cm)
    c = (L + pad) // q
    G, R = SSD_GROUPS, SSD_HEADS // SSD_GROUPS
    xs = x.reshape(b, c, q, G, R, SSD_HEAD_DIM)
    dts = dt.reshape(b, c, q, G, R)
    Bs = Bm.reshape(b, c, q, G, SSD_STATE)
    Cs = Cm.reshape(b, c, q, G, SSD_STATE)
    a_cs = jnp.moveaxis(jnp.cumsum(dts * A.reshape(G, R), axis=2), 2, -1)
    causal = jnp.tril(jnp.ones((q, q), bool))
    decay_in = jnp.exp(jnp.where(causal, a_cs[..., :, None] - a_cs[..., None, :], -jnp.inf))
    xdt = xs * dts[..., None]
    cb = jnp.einsum('bcqgn,bckgn->bcgqk', Cs, Bs)
    y_diag = jnp.einsum('bcgqk,bcgrqk,bckgrp->bcqgrp', cb, decay_in, xdt)
    decay_to_end = jnp.exp(a_cs[..., -1:] - a_cs)
    chunk_states = jnp.einsum('bckgn,bcgrk,bckgrp->bcgrpn', Bs, decay_to_end, xdt)
    chunk_decay = jnp.exp(a_cs[..., -1])

    def step(h, inp):
        dec, st = inp
        return h * dec[..., None, None] + st, h

    h_final, h_prev = lax.scan(step, h0.reshape(b, G, R, SSD_HEAD_DIM, SSD_STATE),
                               (jnp.moveaxis(chunk_decay, 1, 0), jnp.moveaxis(chunk_states, 1, 0)))
    h_prev = jnp.moveaxis(h_prev, 0, 1)
    y_off = jnp.einsum('bcqgn,bcgrpn,bcgrq->bcqgrp', Cs, h_prev, jnp.exp(a_cs))
    y = (y_diag + y_off).reshape(b, c * q, SSD_HEADS, SSD_HEAD_DIM)[:, :L]
    return y, h_final.reshape(b, SSD_HEADS, SSD_HEAD_DIM, SSD_STATE)

def _sink_attend(q, k, v, mask, sinks):
    f32 = jnp.float32
    s = jnp.einsum('bnqhrd,bnkhd->bnhrqk', q.astype(f32), k.astype(f32)) * (ATT_HEAD_DIM ** -0.5)
    s = jnp.where(mask[None, :, None, None], s, NEG_INF)
    sink = sinks.astype(f32).reshape(1, 1, ATT_KV_HEADS, ATT_REP, 1, 1)
    m = jnp.maximum(jnp.max(s, axis=-1, keepdims=True), sink)
    p = jnp.exp(s - m)
    p = p / (jnp.sum(p, axis=-1, keepdims=True) + jnp.exp(sink - m))
    o = jnp.einsum('bnhrqk,bnkhd->bnqhrd', p, v.astype(f32))
    b, n, Q = o.shape[:3]
    return o.reshape(b, n * Q, Q_DIM)

def _swa_prompt(q, k, v, sinks):
    b, L = q.shape[:2]
    nb = L // WINDOW
    qb = q.reshape(b, nb, WINDOW, ATT_KV_HEADS, ATT_REP, ATT_HEAD_DIM)

    def band(t):
        tb = t.reshape(b, nb, WINDOW, ATT_KV_HEADS, ATT_HEAD_DIM)
        prev = jnp.concatenate([jnp.zeros_like(tb[:, :1]), tb[:, :-1]], axis=1)
        return jnp.concatenate([prev, tb], axis=2)

    qi = jnp.arange(WINDOW)[:, None]
    kj = jnp.arange(2 * WINDOW)[None, :]
    rel = qi + WINDOW - kj
    blk = jnp.arange(nb)[:, None, None]
    mask = ((rel >= 0) & (rel <= WINDOW))[None] & ((blk > 0) | (kj >= WINDOW)[None])
    return _sink_attend(qb, band(k), band(v), mask, sinks)

def _swa_cached(q, k, v, kbuf, vbuf, sinks):
    b, L = q.shape[:2]
    wc = kbuf.shape[1]
    kc = jnp.concatenate([kbuf.astype(k.dtype), k], axis=1)
    vc = jnp.concatenate([vbuf.astype(v.dtype), v], axis=1)
    qi = jnp.arange(L)[:, None]
    kj = jnp.arange(wc + L)[None, :]
    rel = qi + wc - kj
    mask = ((rel >= 0) & (rel <= WINDOW))[None]
    o = _sink_attend(q.reshape(b, 1, L, ATT_KV_HEADS, ATT_REP, ATT_HEAD_DIM), kc[:, None], vc[:, None], mask, sinks)
    return o, kc[:, -wc:], vc[:, -wc:]

def _ssd_swa_mixer(h, ssm0, conv0, kbuf, vbuf, w_in, conv_w, conv_b, dt_bias, a_log, d_skip,
                   ssd_norm, q_norm, k_norm, sinks, w_out):
    f32 = jnp.float32
    b, L, _ = h.shape
    proj = h @ w_in
    cuts = np.cumsum([SSD_WIDTH, CONV_DIM, SSD_HEADS, Q_DIM, KV_DIM]).tolist()
    z, xbc, dt_raw, q, k, v = jnp.split(proj, cuts, axis=-1)
    xbc, conv1 = _causal_conv(xbc, conv0, conv_w, conv_b)
    xs, Bm, Cm = jnp.split(xbc, [SSD_WIDTH, SSD_WIDTH + SSD_GROUPS * SSD_STATE], axis=-1)
    dt = jax.nn.softplus(dt_raw.astype(f32) + dt_bias.astype(f32))
    A = -jnp.exp(a_log.astype(f32))
    xh = xs.reshape(b, L, SSD_HEADS, SSD_HEAD_DIM).astype(f32)
    y, ssm1 = _ssd_scan(xh, dt, A,
                        Bm.reshape(b, L, SSD_GROUPS, SSD_STATE).astype(f32),
                        Cm.reshape(b, L, SSD_GROUPS, SSD_STATE).astype(f32),
                        ssm0.astype(f32))
    y = (y + xh * d_skip.astype(f32)[:, None]).reshape(b, L, SSD_WIDTH) * jax.nn.silu(z.astype(f32))
    yg = y.reshape(b, L, SSD_GROUPS, SSD_WIDTH // SSD_GROUPS)
    yg = yg * lax.rsqrt(jnp.mean(yg * yg, axis=-1, keepdims=True) + RMS_EPS)
    y_ssd = (yg.reshape(b, L, SSD_WIDTH) * ssd_norm.astype(f32)).astype(h.dtype)
    q = _rms(q.reshape(b, L, ATT_HEADS, ATT_HEAD_DIM), q_norm)
    k = _rms(k.reshape(b, L, ATT_KV_HEADS, ATT_HEAD_DIM), k_norm)
    v = v.reshape(b, L, ATT_KV_HEADS, ATT_HEAD_DIM)
    if kbuf is None:
        o = _swa_prompt(q, k, v, sinks)
        k1, v1 = k[:, -WINDOW:], v[:, -WINDOW:]
    else:
        o, k1, v1 = _swa_cached(q, k, v, kbuf, vbuf, sinks)
    out = jnp.concatenate([y_ssd, o.astype(h.dtype)], axis=-1) @ w_out
    return out, ssm1, conv1, k1, v1

def _rwkv7_mixer(h, wkv0, shift0, mu, w0, w1, w2, a0, a1, a2, g1, g2, kk_coef, ka, rk,
                 wr, wk, wv, wo, ln_w, ln_b):
    f32 = jnp.float32
    b, L, _ = h.shape
    prev = jnp.concatenate([shift0[:, None].astype(h.dtype), h[:, :-1]], axis=1)
    xx = prev - h
    xr, xw, xk, xv, xa, xg = [h + xx * mu[i] for i in range(6)]
    r = xr @ wr
    k = xk @ wk
    v = xv @ wv
    w_log = -jax.nn.softplus(-(w0 + jnp.tanh(xw @ w1) @ w2).astype(f32)) - 0.5
    decay = jnp.exp(-jnp.exp(w_log))
    a = jax.nn.sigmoid((a0 + (xa @ a1) @ a2).astype(f32))
    g = jax.nn.sigmoid(xg @ g1) @ g2
    hs = lambda t: t.astype(f32).reshape(b, L, RWKV_HEADS, RWKV_HEAD)
    kk = hs(k * kk_coef)
    kk = kk / jnp.maximum(jnp.sqrt(jnp.sum(kk * kk, axis=-1, keepdims=True)), 1e-12)
    k = hs(k.astype(f32) * (1.0 + (a - 1.0) * ka.astype(f32)))
    r, decay, v, a = hs(r), hs(decay), hs(v), hs(a)
    tm = lambda t: jnp.moveaxis(t, 1, 0)

    def step(S, inp):
        r_t, w_t, k_t, v_t, a_t, b_t = inp
        sa = jnp.einsum('bhvk,bhk->bhv', S, a_t)
        S = S * w_t[:, :, None, :] + sa[..., None] * b_t[:, :, None, :] + v_t[..., None] * k_t[:, :, None, :]
        return S, jnp.einsum('bhvk,bhk->bhv', S, r_t)

    S1, y = lax.scan(step, wkv0.astype(f32), (tm(r), tm(decay), tm(k), tm(v), tm(-kk), tm(kk * a)))
    y = jnp.moveaxis(y, 0, 1)
    mean = jnp.mean(y, axis=-1, keepdims=True)
    var = jnp.mean((y - mean) ** 2, axis=-1, keepdims=True)
    y = (y - mean) * lax.rsqrt(var + RWKV_GN_EPS)
    y = y * ln_w.astype(f32).reshape(RWKV_HEADS, RWKV_HEAD) + ln_b.astype(f32).reshape(RWKV_HEADS, RWKV_HEAD)
    y = y + jnp.sum(r * k * rk.astype(f32), axis=-1, keepdims=True) * v
    out = (y.reshape(b, L, D_MODEL) * g.astype(f32)).astype(h.dtype) @ wo
    return out, S1, h[:, -1]

def _moe(h, router, wg, wu, wd):
    f32 = jnp.float32
    logits = jnp.einsum('bld,de->ble', h.astype(f32), router.astype(f32))
    top_v, top_i = lax.top_k(logits, TOP_K)
    gates = jax.nn.softmax(top_v, axis=-1)
    combine = jnp.einsum('blk,blke->ble', gates, jax.nn.one_hot(top_i, N_EXPERTS, dtype=f32))
    y = jnp.zeros(h.shape, f32)
    for e in range(N_EXPERTS):
        y = y + combine[..., e:e + 1] * _swiglu(h, wg[e], wu[e], wd[e]).astype(f32)
    return y.astype(h.dtype)

def _trunk(x, ssm, conv, ck, cv, wkv, shift, W):
    n_ssm, n_conv, n_k, n_v, n_wkv, n_shift = [], [], [], [], [], []
    ie = 0
    io = 0
    for layer in range(DEPTH):
        h = _rms(x, W['norm_mix'][layer])
        if layer % 2 == 0:
            out, s1, c1, k1, v1 = _ssd_swa_mixer(
                h, ssm[ie], conv[ie], None if ck is None else ck[ie], None if cv is None else cv[ie],
                W['w_in'][ie], W['conv_w'][ie], W['conv_b'][ie], W['dt_bias'][ie], W['a_log'][ie],
                W['d_skip'][ie], W['ssd_norm'][ie], W['q_norm'][ie], W['k_norm'][ie],
                W['attn_sinks'][ie], W['w_out'][ie])
            x = x + out
            x = x + _swiglu(_rms(x, W['norm_ffn'][layer]), W['ffn_gate'][ie], W['ffn_up'][ie], W['ffn_down'][ie])
            n_ssm.append(s1); n_conv.append(c1); n_k.append(k1); n_v.append(v1)
            ie += 1
        else:
            out, S1, sh1 = _rwkv7_mixer(
                h, wkv[io], shift[io], W['rwkv_mu'][io], W['rwkv_w0'][io], W['rwkv_w1'][io], W['rwkv_w2'][io],
                W['rwkv_a0'][io], W['rwkv_a1'][io], W['rwkv_a2'][io], W['rwkv_g1'][io], W['rwkv_g2'][io],
                W['rwkv_kk'][io], W['rwkv_ka'][io], W['rwkv_rk'][io], W['rwkv_wr'][io], W['rwkv_wk'][io],
                W['rwkv_wv'][io], W['rwkv_wo'][io], W['rwkv_ln_w'][io], W['rwkv_ln_b'][io])
            x = x + out
            x = x + _moe(_rms(x, W['norm_ffn'][layer]), W['moe_router'][io], W['moe_gate'][io],
                         W['moe_up'][io], W['moe_down'][io])
            n_wkv.append(S1); n_shift.append(sh1)
            io += 1
    return (x, jnp.stack(n_ssm), jnp.stack(n_conv), jnp.stack(n_k), jnp.stack(n_v),
            jnp.stack(n_wkv), jnp.stack(n_shift))

def setup_inputs(seed: int = 0) -> dict:
    key = jax.random.key(seed)
    ks = iter(jax.random.split(key, 64))
    f32 = jnp.float32
    nrm = lambda shape, scale: jax.random.normal(next(ks), shape, f32) * scale
    gain = lambda shape: 1.0 + nrm(shape, 0.02)
    unif = lambda shape, lo, hi: jax.random.uniform(next(ks), shape, f32, lo, hi)
    E, O = N_EVEN, N_ODD
    wc = min(WINDOW, PAST_LEN)
    dt0 = jnp.exp(unif((E, SSD_HEADS), math.log(1e-3), math.log(1e-1)))
    dt_bias = dt0 + jnp.log(-jnp.expm1(-dt0))
    return {
        'x_prompt': nrm((BATCH, SEQ, D_MODEL), 1.0),
        'x_sample': nrm((DEC_BATCH, DEC_SEQ, D_MODEL), 1.0),
        'state_ssm': nrm((E, DEC_BATCH, SSD_HEADS, SSD_HEAD_DIM, SSD_STATE), 0.1),
        'state_conv': nrm((E, DEC_BATCH, SSD_CONV - 1, CONV_DIM), 1.0),
        'cache_swa_k': nrm((E, DEC_BATCH, wc, ATT_KV_HEADS, ATT_HEAD_DIM), 1.0),
        'cache_swa_v': nrm((E, DEC_BATCH, wc, ATT_KV_HEADS, ATT_HEAD_DIM), 1.0),
        'state_wkv': nrm((O, DEC_BATCH, RWKV_HEADS, RWKV_HEAD, RWKV_HEAD), 0.1),
        'state_shift': nrm((O, DEC_BATCH, D_MODEL), 1.0),
        'norm_mix': gain((DEPTH, D_MODEL)),
        'norm_ffn': gain((DEPTH, D_MODEL)),
        'w_in': nrm((E, D_MODEL, IN_DIM), D_MODEL ** -0.5),
        'conv_w': nrm((E, SSD_CONV, CONV_DIM), SSD_CONV ** -0.5),
        'conv_b': nrm((E, CONV_DIM), 0.02),
        'dt_bias': dt_bias,
        'a_log': jnp.log(unif((E, SSD_HEADS), 1.0, 16.0)),
        'd_skip': gain((E, SSD_HEADS)),
        'ssd_norm': gain((E, SSD_WIDTH)),
        'q_norm': gain((E, ATT_HEAD_DIM)),
        'k_norm': gain((E, ATT_HEAD_DIM)),
        'attn_sinks': nrm((E, ATT_HEADS), 0.5),
        'w_out': nrm((E, MIX_DIM, D_MODEL), MIX_DIM ** -0.5),
        'ffn_gate': nrm((E, D_MODEL, D_FF), D_MODEL ** -0.5),
        'ffn_up': nrm((E, D_MODEL, D_FF), D_MODEL ** -0.5),
        'ffn_down': nrm((E, D_FF, D_MODEL), D_FF ** -0.5),
        'rwkv_mu': unif((O, 6, D_MODEL), 0.0, 1.0),
        'rwkv_w0': unif((O, D_MODEL), -6.0, -1.0),
        'rwkv_w1': nrm((O, D_MODEL, DECAY_LORA), 0.1 * D_MODEL ** -0.5),
        'rwkv_w2': nrm((O, DECAY_LORA, D_MODEL), 0.1 * DECAY_LORA ** -0.5),
        'rwkv_a0': nrm((O, D_MODEL), 0.1),
        'rwkv_a1': nrm((O, D_MODEL, ICLR_LORA), 0.1 * D_MODEL ** -0.5),
        'rwkv_a2': nrm((O, ICLR_LORA, D_MODEL), 0.1 * ICLR_LORA ** -0.5),
        'rwkv_g1': nrm((O, D_MODEL, GATE_LORA), D_MODEL ** -0.5),
        'rwkv_g2': nrm((O, GATE_LORA, D_MODEL), GATE_LORA ** -0.5),
        'rwkv_kk': 0.85 + nrm((O, D_MODEL), 0.02),
        'rwkv_ka': gain((O, D_MODEL)),
        'rwkv_rk': nrm((O, RWKV_HEADS, RWKV_HEAD), 0.1),
        'rwkv_wr': nrm((O, D_MODEL, D_MODEL), D_MODEL ** -0.5),
        'rwkv_wk': nrm((O, D_MODEL, D_MODEL), D_MODEL ** -0.5),
        'rwkv_wv': nrm((O, D_MODEL, D_MODEL), D_MODEL ** -0.5),
        'rwkv_wo': nrm((O, D_MODEL, D_MODEL), D_MODEL ** -0.5),
        'rwkv_ln_w': gain((O, D_MODEL)),
        'rwkv_ln_b': nrm((O, D_MODEL), 0.02),
        'moe_router': nrm((O, D_MODEL, N_EXPERTS), D_MODEL ** -0.5),
        'moe_gate': nrm((O, N_EXPERTS, D_MODEL, EXPERT_FF), D_MODEL ** -0.5),
        'moe_up': nrm((O, N_EXPERTS, D_MODEL, EXPERT_FF), D_MODEL ** -0.5),
        'moe_down': nrm((O, N_EXPERTS, EXPERT_FF, D_MODEL), EXPERT_FF ** -0.5),
    }

def reference(x_prompt, x_sample, state_ssm, state_conv, cache_swa_k, cache_swa_v, state_wkv, state_shift,
              norm_mix, norm_ffn, w_in, conv_w, conv_b, dt_bias, a_log, d_skip, ssd_norm, q_norm, k_norm,
              attn_sinks, w_out, ffn_gate, ffn_up, ffn_down, rwkv_mu, rwkv_w0, rwkv_w1, rwkv_w2, rwkv_a0,
              rwkv_a1, rwkv_a2, rwkv_g1, rwkv_g2, rwkv_kk, rwkv_ka, rwkv_rk, rwkv_wr, rwkv_wk, rwkv_wv, rwkv_wo,
              rwkv_ln_w, rwkv_ln_b, moe_router, moe_gate, moe_up, moe_down):
    W = dict(norm_mix=norm_mix, norm_ffn=norm_ffn, w_in=w_in, conv_w=conv_w, conv_b=conv_b, dt_bias=dt_bias,
             a_log=a_log, d_skip=d_skip, ssd_norm=ssd_norm, q_norm=q_norm, k_norm=k_norm, attn_sinks=attn_sinks,
             w_out=w_out, ffn_gate=ffn_gate, ffn_up=ffn_up, ffn_down=ffn_down, rwkv_mu=rwkv_mu, rwkv_w0=rwkv_w0,
             rwkv_w1=rwkv_w1, rwkv_w2=rwkv_w2, rwkv_a0=rwkv_a0, rwkv_a1=rwkv_a1, rwkv_a2=rwkv_a2, rwkv_g1=rwkv_g1,
             rwkv_g2=rwkv_g2, rwkv_kk=rwkv_kk, rwkv_ka=rwkv_ka, rwkv_rk=rwkv_rk, rwkv_wr=rwkv_wr, rwkv_wk=rwkv_wk,
             rwkv_wv=rwkv_wv, rwkv_wo=rwkv_wo, rwkv_ln_w=rwkv_ln_w, rwkv_ln_b=rwkv_ln_b, moe_router=moe_router,
             moe_gate=moe_gate, moe_up=moe_up, moe_down=moe_down)
    bp = x_prompt.shape[0]
    z_ssm = jnp.zeros((N_EVEN, bp) + state_ssm.shape[2:], jnp.float32)
    z_conv = jnp.zeros((N_EVEN, bp) + state_conv.shape[2:], x_prompt.dtype)
    z_wkv = jnp.zeros((N_ODD, bp) + state_wkv.shape[2:], jnp.float32)
    z_shift = jnp.zeros((N_ODD, bp) + state_shift.shape[2:], x_prompt.dtype)
    y_prompt, p_ssm, p_conv, p_k, p_v, p_wkv, p_shift = _trunk(
        x_prompt, z_ssm, z_conv, None, None, z_wkv, z_shift, W)
    y_sample, s_ssm, s_conv, s_k, s_v, s_wkv, s_shift = _trunk(
        x_sample, state_ssm, state_conv, cache_swa_k, cache_swa_v, state_wkv, state_shift, W)
    return (y_prompt, y_sample, p_ssm, p_conv, p_k, p_v, p_wkv, p_shift,
            s_ssm, s_conv, s_k, s_v, s_wkv, s_shift)


_drawn_inputs = setup_inputs


def setup_inputs(seed=0):
    import zlib

    import numpy as np

    out = dict(_drawn_inputs(seed))
    spreads = {}
    factors = {'d_skip': 4.337,
     'q_norm': 4.426,
     'k_norm': 2.847,
     'attn_sinks': 5.685,
     'rwkv_w1': 8.0,
     'rwkv_w2': 8.0,
     'rwkv_a1': 4.982,
     'rwkv_a2': 4.982,
     'rwkv_ln_b': 2.733}
    for name, (base, spread) in spreads.items():
        noise = np.random.default_rng([zlib.crc32(name.encode()), seed]).standard_normal(out[name].shape)
        drawn = base * np.exp(spread * noise) if base else spread * noise
        out[name] = __import__('jax').numpy.asarray(drawn.astype(out[name].dtype))
    for name, factor in factors.items():
        out[name] = (out[name] * factor).astype(out[name].dtype)
    return out
```

```python
import numpy as np
from contextlib import ExitStack
import concourse.bass as bass
from concourse import mybir

F32 = mybir.dt.float32
F32R = mybir.dt.float32r
U32 = mybir.dt.uint32
I32 = mybir.dt.int32
ALU = mybir.AluOpType
ACT = mybir.ActivationFunctionType
AX = mybir.AxisListType.X

P = 128
D = 1024
KT = D // P
TP = 256
DB, DL = 8, 4
TS = DB * DL
T = TP + TS
NH = 16
HD = 64
CONV = 1536
CT = CONV // P
NKV = 4
FF = 2816
NE = 8
EPS = 1e-6
GN_EPS = 64e-5
NEG = -1e30
RING = 3
SLOT = 6144
FC = FF // 256
C_DECAY = float(np.exp(-0.5))
TOK = [(0, 128), (128, 128), (256, 32)]

CONST_COLS = {}


def const_table():
    cols, at = [], 0

    def put(name, a):
        nonlocal at
        full = np.zeros((P, a.shape[1]), np.float32)
        full[:a.shape[0]] = a
        cols.append(full)
        CONST_COLS[name] = (at, a.shape[1])
        at += a.shape[1]

    i = np.arange(P)
    k, q = i[:, None], i[None, :]
    put("ident", np.eye(P))
    put("ones", np.ones((P, P)))
    put("blk64", (k // 64 == q // 64) * 1.0)
    put("tri", (k <= q) * 1.0)
    s = np.arange(TS)
    sk, sq = s[:, None], s[None, :]
    same = sk // DL == sq // DL
    put("tris", (same & (sk <= sq)) * 1.0)
    put("bmask", (np.arange(64)[:, None] % TS // DL == np.arange(DB)[None]) * 1.0)
    c64 = k // 64 == q // 64
    put("m4", np.concatenate([c64 & (k < q), c64 & (k <= q), c64 & (k < q), c64 & (k <= q)], 1) * 1.0)
    put("low", (c64 & (k > q)) * 1.0)
    put("m4s", np.concatenate([same & (sk < sq), same & (sk <= sq)] * 2, 1) * 1.0)
    put("lows", (same & (sk > sq)) * 1.0)
    for lv in range(6):
        b = 1 << lv
        put(f"lev{lv}", ((k // (2 * b) == q // (2 * b)) & (k // b > q // b)) * 1.0)
    put("lev0u", ((k // 2 == q // 2) & (k < q)) * 1.0)
    put("strict", (k < q) * 1.0)
    put("iota", np.tile(np.arange(P), (P, 1)) * 1.0)
    r1 = np.ones(T)
    r1[[0, 128]] = 0
    r1[TP::DL] = 0
    put("reset128", np.tile(r1, (16, 1)))
    r2 = np.ones(T)
    r2[[0, 64, 128, 192]] = 0
    r2[TP::DL] = 0
    put("reset64", np.tile(r2, (P, 1)))
    return np.concatenate(cols, 1).astype(np.float32)


def attn_table():
    i = np.arange(P)
    k, q = np.arange(P)[None], i[:, None]
    a0 = np.where(k <= q, 0, NEG)
    k2 = np.arange(256)[None]
    rel = q + 128 - k2
    a1 = np.where((rel >= 0) & (rel <= 128), 0, NEG)
    r = i
    b2, l = r // 64, r % 4
    out = [a0, a1]
    for jj in range(4):
        b = 2 * jj + b2
        old = np.where(k >= l[:, None], 0, NEG)
        c = np.arange(TS)[None]
        new = np.where((c // DL == b[:, None]) & (c % DL <= l[:, None]), 0, NEG)
        out += [old, new]
    return np.concatenate(out, 1).astype(np.float32)


CONSTS = const_table()
ATTN_MASKS = attn_table()
VEC = {}


def vec_cols():
    at = 0
    for name, n in (("nm0", 8), ("nf0", 8), ("nm1", 8), ("nf1", 8), ("ssdn", 8), ("convw", 48), ("convb", 12),
                    ("dskip", 8), ("qn", 1), ("kn", 1), ("mu", 48), ("w0", 8), ("a0", 8), ("kk", 8), ("ka", 8),
                    ("rk", 8), ("lnw", 8), ("lnb", 8), ("sinks", 16), ("sinkrow", 1), ("dtb", 1), ("alog", 1)):
        VEC[name] = (at, n)
        at += n
    return at


NVEC = vec_cols()
W_IN_CHUNKS = [(0, 768), (768, 768), (1536, 768), (2304, 272), (2576, 768), (3344, 768)]
W_OUT_CHUNKS = [(0, 384), (384, 384), (768, 256)]


def decoder_trunk(nc, a, out):
    with ExitStack() as ctx:
        def sb(name, n, dt=F32, parts=P):
            return ctx.enter_context(nc.sbuf_tensor(name, [parts, n], dt))

        sems = {}

        def sem(name):
            if name not in sems:
                sems[name] = ctx.enter_context(nc.semaphore(name))
            return sems[name]

        xb = sb("x", KT * T)
        cst = sb("cst", CONSTS.shape[1])
        vec = sb("vec", NVEC + 8)
        rt = sb("router", KT * NE)
        rs_ = sb("rs", 2 * T)
        rs = [rs_[:, i * T:(i + 1) * T] for i in range(2)]
        shiftst = sb("shiftst", KT * DB)[:, :].rearrange("p (k b) -> p k b", b=DB)
        ps = ctx.enter_context(nc.psum_tensor("ps", [P, 8, 512], F32))
        with nc.sbuf_tensor("ring", [P, RING * SLOT], F32) as ring, nc.sbuf_tensor("h", [P, KT * T], F32) as hb:
            ARENA = (nc.sbuf_bytes_remaining - 64) // 4
            with nc.sbuf_tensor("arena", [P, ARENA], F32) as ar:
                pass
        MS, GU = 4, 4096
        rest_ring, hsel_, rest_arena = sb("rest_ring", RING * SLOT, F32R), sb("hsel", KT * T, F32R), sb("rest_arena", SLOT, F32R)
        mhead_, actTm_ = sb("head", 2 * SLOT, F32R), sb("actT_split", 1024, F32R)
        moe = sb("moe", ARENA - 3 * SLOT - 1024)

        def C(name, rows=P):
            o, n = CONST_COLS[name]
            return cst[0:rows, o:o + n]

        def v(name, j=0, r0=0, r1=P):
            o, n = VEC[name]
            return vec[r0:r1, o + j:o + j + 1]

        x = xb[:, :].rearrange("p (k t) -> p k t", t=T)
        h = hb[:, :].rearrange("p (k t) -> p k t", t=T)
        ident = C("ident")
        kn8 = vec[:, NVEC:NVEC + 1]

        def slot(n, w=SLOT):
            s = n % RING
            return ring[:, s * SLOT:s * SLOT + w]

        pos = [0]

        def area(n):
            o = pos[0]
            pos[0] += n
            assert pos[0] <= ARENA, (pos[0], ARENA)
            return ar[:, o:o + n]

        def moe_area(n):
            o = pos[0]
            pos[0] += n
            assert pos[0] <= ARENA - 3 * SLOT - 1024, pos[0]
            return moe[:, o:o + n]

        z = area(KT * T).rearrange("p (k t) -> p k t", t=T)
        xc = area(CT * T).rearrange("p (k t) -> p k t", t=T)
        qT = area(KT * T).rearrange("p (k t) -> p k t", t=T)
        kT = area(NKV * T).rearrange("p (k t) -> p k t", t=T)
        vtok = area(3 * 256).rearrange("p (c n) -> p c n", c=3)
        padw = 3 + TP + DB * 7
        pads_area = area(max(6 * padw, 2048))
        pad = [pads_area[:, i * padw:(i + 1) * padw] for i in range(4)]
        ctmp = [pads_area[:, (4 + i) * padw:(5 + i) * padw] for i in range(2)]
        Bm = pads_area[:, 0:2048].rearrange("p (b n) -> p b n", b=DB)
        convout = area(CT * 27).rearrange("p (k n) -> p k n", n=27)
        convst = area(CT * 24).rearrange("p (k n) -> p k n", n=24)
        SC = area(T)
        acs = area(T)
        TM = area(3 * 96).rearrange("p (c n) -> p c n", c=3)
        xdt_area = area(2 * 3 * D)
        xdt = xdt_area[:, 0:3 * D].rearrange("p (c n) -> p c n", c=3)
        xdec = xdt_area[:, 3 * D:6 * D].rearrange("p (c n) -> p c n", c=3)
        qksq = xdt_area[:, 0:12 * T].rearrange("p (k t) -> p k t", t=T)
        ysq = xdt_area[:, 0:KT * T].rearrange("p (k t) -> p k t", t=T)
        oT = xdt_area[:, 0:KT * T].rearrange("p (k t) -> p k t", t=T)
        PT = [xdt_area[:, KT * T + i * 1536:KT * T + (i + 1) * 1536] for i in range(2)]
        PP = [xc[:, :, :].rearrange("p k t -> p (k t)")[:, i * 1536:(i + 1) * 1536] for i in range(2)]
        Btok = area(768).rearrange("p (c n) -> p c n", c=3)
        eb_area = area(2048 + 1024 + 1024)
        Eb = [eb_area[:, i * 512:(i + 1) * 512] for i in range(4)]
        expq = [eb_area[:, 2048 + i * 512:2560 + i * 512] for i in range(2)]
        abq = [eb_area[:, 3072 + i * 512:3584 + i * 512] for i in range(2)]
        dtt = [eb_area[0:16, i * T:(i + 1) * T] for i in range(8)]
        CsS = area(512).rearrange("p (h t) -> p h t", t=TS)
        am = area(ATTN_MASKS.shape[1])
        dend = hb[:, 2112:2128]
        dsm = hb[:, 2128:2256].rearrange("p (h b) -> p h b", b=DB)
        stats = area(64)
        CBm = hb[:, 0:512].rearrange("p (c g q) -> p c g q", c=2, g=2)
        CBs = hb[0:TS, 512:576].rearrange("p (g q) -> p g q", g=2)
        H1T = hb[:, 576:1600]
        Ms = hb[0:TS, 1600:2112].rearrange("p (h t) -> p h t", t=TS)
        SA = eb_area[:, 0:512]
        SBn = eb_area[0:TS, 512:1024]
        PS = eb_area[:, 1024:1664].rearrange("p (j k) -> p j k", k=160)
        PTA = eb_area[:, 2048:2560]
        PTB = eb_area[0:TS, 2560:3072]
        sq0 = z
        sg = [eb_area[:, i * T:(i + 1) * T] for i in range(2)]
        prod = [eb_area[:, (2 + i) * T:(3 + i) * T] for i in range(4)]
        sq2 = xc
        sq3 = eb_area[:, 6 * T:14 * T].rearrange("p (k t) -> p k t", t=T)
        hsplit = [rest_arena[:, 0:KT * T].rearrange("p (k t) -> p k t", t=T), hsel_[:, :].rearrange("p (k t) -> p k t", t=T)]
        actT = [[rest_arena[:, (KT + 2 * i + u) * T:(KT + 2 * i + u + 1) * T] for u in range(2)] for i in range(4)]
        L0_END = pos[0]

        pos[0] = 0
        xx = area(KT * T).rearrange("p (k t) -> p k t", t=T)
        xi2 = area(2 * KT * T)
        xi = [xi2[:, i * KT * T:(i + 1) * KT * T].rearrange("p (k t) -> p k t", t=T) for i in range(2)]
        AR = xi2[:, :].rearrange("p (k a t) -> p k a t", k=KT, a=2)
        rT = area(KT * T).rearrange("p (k t) -> p k t", t=T)
        k1 = area(KT * T).rearrange("p (k t) -> p k t", t=T)
        vT = area(KT * T).rearrange("p (k t) -> p k t", t=T)
        sw = area(KT * T).rearrange("p (k t) -> p k t", t=T)
        aT = area(KT * T).rearrange("p (k t) -> p k t", t=T)
        gT = area(KT * T).rearrange("p (k t) -> p k t", t=T)
        A4 = area(8 * 512).rearrange("p (h a t) -> p h a t", h=8, a=4)
        Us = area(512)
        Pend = area(KT * 12).rearrange("p (k n) -> p k n", n=12)
        tm1 = [area(T) for _ in range(2)]
        shiftout = area(KT * 9).rearrange("p (k b) -> p k b", b=9)
        omka = area(8)
        hid = tm1
        xxf = xx[:, :, :].rearrange("p k t -> p (k t)")
        v1 = xxf[:, 0:1024]
        b1 = xxf[:, 1024:2048]
        k1t = hb[:, 0:1024]
        St = hb[:, 1024:1536]
        Zs = hb[:, 1536:2048]
        yT = sw
        SCR = 1
        scr = ring[:, SCR * SLOT:(SCR + 1) * SLOT]
        Mi, Mti, Xt, Xl, Yi = [scr[:, i * 1024:(i + 1) * 1024].rearrange("p (h t) -> p h t", t=P) for i in range(5)]
        M2, Mt2, Xt2, Xl2, Yi2 = [scr[0:TS, i * 1024:i * 1024 + 512].rearrange("p (h t) -> p h t", t=TS) for i in range(5)]
        Zs2 = scr[0:TS, 5120:6144]
        Sd = scr[:, 5120:6144].rearrange("p (k r v) -> p k r v", k=KT, r=2)
        UVm = [scr[0:64, 4096 + i * 512:4608 + i * 512].rearrange("p (b v) -> p b v", b=DB) for i in range(2)]
        A4f = A4[:, :, :, :].rearrange("p h a t -> p (h a t)")
        A4s = A4f[0:TS, 0:2048].rearrange("p (h a t) -> p h a t", h=NH, a=4)
        UV = A4f[0:64, 2048:3072]
        BK = A4f[0:64, 3072:4096]
        z1T = Us[:, 0:256].rearrange("p (k t) -> p k t", t=TS)
        y1 = Us[:, 256:512].rearrange("p (k t) -> p k t", t=TS)

        pos[0] = 0
        mslot = [slot(1), slot(0), slot(2), ar[:, 0:SLOT]]
        mrest = [rest_ring[:, i * SLOT:(i + 1) * SLOT] for i in (1, 0, 2)] + [rest_arena[:, :]]
        mhead = [mhead_[:, i * SLOT:(i + 1) * SLOT] for i in range(2)]
        htok = moe_area(3 * D).rearrange("p (c n) -> p c n", c=3)
        hsel = [hsel_[:, i * 1024:(i + 1) * 1024].rearrange("p (k c) -> p k c", k=KT) for i in range(2)]
        ysb = moe_area(D)
        Sel = moe_area(3 * P).rearrange("p (c n) -> p c n", c=3)
        Wsel = moe_area(3 * P).rearrange("p (c n) -> p c n", c=3)
        Wt = moe_area(T)
        sgm = moe_area(256)
        actm = [moe_area(256) for _ in range(2)]
        actTm = [[actTm_[:, (2 * i + u) * 256:(2 * i + u + 1) * 256] for u in range(2)] for i in range(2)]
        lg, mx, ixf, oh1, oh2, comb, selm, rank = [moe_area(24).rearrange("p (c e) -> p c e", c=3) for _ in range(8)]
        ixu = moe_area(24).bitcast(U32).rearrange("p (c e) -> p c e", c=3)
        gt = moe_area(12).rearrange("p (c e) -> p c e", c=3)
        NJ = NE + 4
        rankJ, combJ = [moe_area(3 * (NJ + 1)).rearrange("p (c j) -> p c j", c=3) for _ in range(2)]
        flags, posn, ohx, tmpx, erow = [moe_area(16) for _ in range(5)]
        cntm = moe_area(8)
        cur = moe_area(6).rearrange("p (a c) -> p a c", a=2)
        jobf = moe_area(8)
        jobi = moe_area(8).bitcast(I32)

        const_dram, attn_dram = a["consts"], a["attn_masks"]

        base, order = {}, [0]

        def stage(name, n):
            assert name not in base
            base[name] = order[0]
            order[0] += n

        for name, n in (("N1", 1), ("Z", 8), ("X", 12), ("DT", 1), ("Q", 8), ("K", 4), ("V", 3), ("QN", 12), ("TT", 1),
                        ("XT", 6), ("BT", 2), ("CB", 2), ("H1", 2), ("ES", 1)):
            stage(name, n)
        for qd in range(4):
            stage(f"E{qd}", 2)
            stage(f"Y{qd}", 2)
        for name, n in (("FP", 2), ("FS", 16), ("YN", 2)):
            stage(name, n)
        for j in range(5):
            if j < 4:
                stage(f"S{j}", 4)
            if j > 0:
                stage(f"PT{j - 1}", 3)
                stage(f"O{j - 1}", 2)
        for name, n in (("SS", 4), ("ST", 2), ("PTS", 2), ("OS", 2), ("WO", 8), ("N2", 1)):
            stage(name, n)
        for c in range(FC + 1):
            if c < FC:
                stage(f"FU{c}", 4)
            if c:
                stage(f"FD{c - 1}", 8)
        stage("N3", 1)
        for name in "rkv":
            stage("R" + name, 8)
        for name in "wag":
            stage("H" + name, 1)
            stage("R" + name, 8)
        for name, n in (("KN", 8), ("BO", 8)):
            stage(name, n)
        for c in range(2):
            stage(f"VT{c}", 6)
            for hh in range(2):
                stage(f"A{c}{hh}", 8)
                stage(f"X{c}{hh}", 2)
                for lv in range(1, 6):
                    stage(f"LY{c}{hh}{lv}", 2)
                    stage(f"LM{c}{hh}{lv}", 2)
                    if lv < 5:
                        stage(f"LT{c}{hh}{lv}", 2)
                for cc in range(2):
                    stage(f"q{c}{hh}{cc}", 4)
        for name, n in (("sVT", 6), ("sA", 4), ("sX", 2), ("sL", 2), ("sZY", 1), ("sZ", 2), ("sU", 2), ("sS", 16), ("sY", 1),
                        ("GM", 8), ("GV", 8), ("WR", 8), ("N4", 1), ("HT", 6), ("RL", 1), ("RK", 1)):
            stage(name, n)

        def bank(g):
            return ps[:, g % 8, :]

        def full(eng, g):
            eng.wait_ge(sem(f"bank_full{g % 8}"), g // 8 + 1)

        def fullsem(g):
            return sem(f"bank_full{g % 8}")

        def freesem(g):
            return sem(f"bank_free{g % 8}")

        def emptied(eng, g):
            eng.wait_ge(sem(f"bank_free{g % 8}"), g // 8 + 1)

        items = []

        def item(name, dst, src, after):
            items.append((name, dst, src, after))

        def win(n, w):
            return slot(n, KT * w)

        for c, (c0, w) in enumerate(W_IN_CHUNKS):
            item(f"win{c}", None, a["w_in"][c][:, 0:KT * w], KT * w)
        item("ssm0", None, a["ssmT"][0], 4096)
        item("ssm1", None, a["ssmT"][1], 4096)
        item("kv", None, a["kv_cache"], SLOT)
        for c, (c0, w) in enumerate(W_OUT_CHUNKS):
            item(f"wout{c}", None, a["w_out"][c][:, 0:16 * w], 16 * w)
        for c in range(FC):
            item(f"ffn{c}", None, a["ffn_w"][c], SLOT)
        for nm, src in (("wr", a["wr"]), ("wk", a["wk"]), ("wv", a["wv"])):
            for hf in range(2):
                item(f"{nm}{hf}", None, src[hf], 4096)
        item("lora", None, a["lora"], 5120)
        item("wkv", None, a["wkvT"], 4096)
        item("scratch", None, None, SLOT)
        item("wo0", None, a["wo"][0], 4096)
        item("wo1", None, a["wo"][1], 4096)
        where = {it[0]: n for n, it in enumerate(items)}
        loads_of = []
        cnt = [0] * RING
        for n, it in enumerate(items):
            if it[2] is not None:
                cnt[n % RING] += 1
            loads_of.append(cnt[n % RING])
        slot_loads = list(cnt)
        uses = [len(range(s, FC, MS)) for s in range(MS)]

        def W(name, w=None):
            n = where[name]
            return slot(n, w or items[n][3])

        def loaded(eng, name):
            n = where[name]
            eng.wait_ge(sem(f"slot_loaded{n % RING}"), 16 * loads_of[n])

        last_group = {"win0": base["Z"] + 5, "win1": base["X"] + 3, "win2": base["X"] + 9, "win3": base["DT"],
                      "win4": base["Q"] + 5, "win5": base["V"] + 2, "kv": base["OS"],
                      "wout0": base["WO"] + 2, "wout1": base["WO"] + 5, "wout2": base["WO"] + 7,
                      "lora": base["Rg"] + 7}
        for c in range(FC):
            last_group[f"ffn{c}"] = base[f"FD{c}"] + 7
        for nm in "rkv":
            for hf in range(2):
                last_group[f"w{nm}{hf}"] = base["R" + nm] + 4 * hf + 3
        for hf in range(2):
            last_group[f"wo{hf}"] = base["WR"] + 4 * hf + 3

        NG_L1 = order[0]
        MOE_G0 = (NG_L1 + 7) // 8 * 8
        assert len(sems) == 0

        assert where["scratch"] % RING == SCR
        block = ctx.enter_context(nc.Block())

        @block.sync
        def _(sp):
            sp.dma_start(xb[:, :], a["x_fm"]).then_inc(sem("x_loaded"), 16)
            sp.dma_start(cst[:, :], const_dram).then_inc(sem("cst_loaded"), 16)
            sp.dma_start(vec[:, 0:NVEC], a["vecs"]).then_inc(sem("cst_loaded"), 16)
            sp.dma_start(ring[:, 0:KT * 768], a["w_in"][0]).then_inc(sem("slot_loaded0"), 16)
            sp.dma_start(convst, a["convT"].rearrange("p (k n) -> p k n", n=24)).then_inc(sem("l0_loaded"), 16)
            sp.dma_start(am, attn_dram).then_inc(sem("l0_loaded"), 16)
            sp.dma_start(rt[:, :], a["router"]).then_inc(sem("router_loaded"), 16)
            def load_ffn_down(c):
                if c >= RING:
                    emptied(sp, base[f"FD{c - RING}"] + 7)
                o = (where[f"ffn{c}"] % RING) * SLOT
                sp.dma_start(ring[:, o + GU:o + SLOT], a["ffn_w"][c][:, GU:SLOT]).then_inc(sem(f"ffn_down_loaded{c % RING}"), 16)

            for n, (name, _, src, w) in enumerate(items):
                if n == 0:
                    continue
                if name.startswith("ffn") and int(name[3:]) >= RING:
                    c = int(name[3:])
                    emptied(sp, base[f"FU{c - RING}"] + 3)
                    sp.dma_start(slot(n, GU), src[:, 0:GU]).then_inc(sem(f"slot_loaded{n % RING}"), 16)
                    load_ffn_down(c - 1)
                    if c == FC - 1:
                        load_ffn_down(c)
                    continue
                if n >= RING:
                    prev = items[n - RING][0]
                    if prev == "ssm0" or prev == "ssm1":
                        sp.wait_ge(sem(f"{prev}_out"), 16)
                    elif prev == "wkv":
                        sp.wait_ge(sem("s_wkv_out"), 16)
                    elif prev == "scratch":
                        emptied(sp, base["sY"])
                    else:
                        emptied(sp, last_group[prev])
                if name.startswith("ffn"):
                    sp.dma_start(slot(n, GU), src[:, 0:GU]).then_inc(sem(f"slot_loaded{n % RING}"), 16)
                    if name != "ffn0":
                        load_ffn_down(int(name[3:]) - 1)
                elif src is not None:
                    sp.dma_start(slot(n, w), src).then_inc(sem(f"slot_loaded{n % RING}"), 16)
                if name == "wr0":
                    sp.dma_start(shiftst, a["shiftT"].rearrange("p (k n) -> p k n", n=DB)).then_inc(sem("shift_loaded"), 16)
            def load_part(j, e, c, part):
                s = c % MS
                o, n = (0, GU) if part == "gu" else (GU, SLOT - GU)
                sp.wait_ge(sem(f"{part}_slot_free{s}"), (uses[s] * j) + c // MS + 1)
                sp.dma_start(mslot[s][:, o:o + n], a["moe_w"][bass.ds(e, 1), c, :, o:o + n].rearrange("a p n -> (a p) n"))\
                    .then_inc(sem(f"{part}_loaded{s}"), 16)

            def load_expert(j, e):
                for c in range(FC + 1):
                    if c < FC:
                        load_part(j, e, c, "gu")
                    if c:
                        load_part(j, e, c - 1, "dn")

            emptied(sp, base["sY"])
            sp.sem_inc(sem("gu_slot_free0"), 1)
            sp.sem_inc(sem("dn_slot_free0"), 1)
            emptied(sp, base["WR"] + 7)
            for s in (1, 2):
                sp.sem_inc(sem(f"gu_slot_free{s}"), 1)
                sp.sem_inc(sem(f"dn_slot_free{s}"), 1)
            emptied(sp, base["N4"])
            sp.sem_inc(sem("gu_slot_free3"), 1)
            sp.sem_inc(sem("dn_slot_free3"), 1)
            with sp.Fori(0, NE) as j:
                load_expert(j, j)
            sp.wait_ge(sem("jobs_ready"), 1)
            njobs = sp.value_load(jobi[0:1, 4:5], min_val=NE, max_val=NJ)
            with sp.If(njobs > NE):
                with sp.Fori(NE, njobs) as j:
                    e = sp.value_load(jobi[0:1, bass.ds(j - NE, 1)], min_val=0, max_val=NE - 1)
                    load_expert(j, e)
            sp.wait_ge(sem("y_final"), 1)
            sp.dma_start(out["y"], xb[:, :]).then_inc(sem("y_stored"), 16)
            sp.wait_ge(sem("y_stored"), 16)

        @block.gpsimd
        def _(pool):
            def store(dst, src):
                pool.dma_start(dst, src).then_inc(sem("l0_stored"), 16)

            for n_, val in enumerate((EPS, HD * EPS, GN_EPS)):
                ins = nc.gpsimd.memset(vec[:, NVEC + 2 + n_:NVEC + 3 + n_], val)
            ins.then_inc(sem("eps_ready"), 1)
            for i in range(4):
                nc.gpsimd.memset(pad[i][:, 0:3], 0.0)
            nc.gpsimd.memset(SC[0:96, :], 0.0).then_inc(sem("pool_cleared"), 1)
            pool.dma_start(out["s_kc"], a["kc_nat"][:, DL:P, :]).then_inc(sem("l0_stored"), 16)
            pool.dma_start(out["s_vc"], a["vc_nat"][:, DL:P, :]).then_inc(sem("l0_stored"), 16)
            pool.wait_ge(sem("l0_loaded"), 32)
            for t in range(CT):
                pd = pad[t % 4]
                sp_ = pd[:, 3 + TP:padw].rearrange("p (b n) -> p b n", n=7)
                if t >= 4:
                    pool.wait_ge(sem("conv_done"), t - 3)
                    pool.wait_ge(sem("tail_saved"), t - 3)
                nc.gpsimd.tensor_copy(sp_[:, :, 0:3], convst[:, t, :].rearrange("p (b n) -> p b n", n=3))\
                    .then_inc(sem("padstate_ready"), 1)
                pool.wait_ge(sem("pad_ready"), t + 1)
                nc.gpsimd.tensor_copy(convout[:, t, 0:3], pd[:, TP:TP + 3])
                nc.gpsimd.tensor_copy(convout[:, t, 3:27].rearrange("p (b n) -> p b n", n=3), sp_[:, :, 4:7])\
                    .then_inc(sem("tail_saved"), 1)
            pool.wait_ge(sem("tail_saved"), CT)
            store(out["conv"].rearrange("p (k n) -> p k n", n=27), convout)
            pool.wait_ge(sem("k_normed"), NKV)
            store(out["kT"].rearrange("p (k n) -> p k n", n=128 + TS), kT[0:64, :, 128:T])
            emptied(pool, base["V"] + 2)
            store(out["v_p"], vtok[:, 1, :])
            store(out["v_s"], vtok[0:TS, 2, :])
            emptied(pool, base["BT"] + 1)
            pool.wait_ge(sem("conv_done"), CT)
            nc.gpsimd.tensor_tensor(Bm[0:TS, :, :], Btok[0:TS, 2, :].unsqueeze(1).broadcast_to([TS, DB, 256]),
                                    C("bmask", TS).unsqueeze(2).broadcast_to([TS, DB, 256]), ALU.mult)\
                .then_inc(sem("Bm_ready"), 1)
            for g in range(2):
                emptied(pool, base[f"Y{2 * g + 1}"] + 1)
                st = W(f"ssm{g}").rearrange("p (b h c) -> p b h c", b=DB, c=HD)
                for b in range(DB):
                    nc.gpsimd.tensor_tensor(st[:, b], st[:, b],
                                            dsm[:, 8 * g:8 * g + 8, b].unsqueeze(2).broadcast_to([P, 8, HD]), ALU.mult)\
                        .then_inc(sem("ssm_decayed"), 1)
            pool.wait_ge(sem("pssm_ready"), 2)
            store(out["p_ssm"], H1T)
            for g in range(2):
                pool.wait_ge(sem("sssm_ready"), DB * (g + 1))
                pool.dma_start(out["s_ssm"][g], W(f"ssm{g}")).then_inc(sem(f"ssm{g}_out"), 16)
            pool.wait_ge(sem("shiftout_ready"), 2)
            pool.dma_start(out["shift"].rearrange("p (k n) -> p k n", n=9), shiftout).then_inc(sem("shift_stored"), 16)
            for c in range(2):
                for hh in range(2):
                    for lv in range(1, 6):
                        if lv > 1:
                            emptied(pool, base[f"LY{c}{hh}{lv - 1}"] + 1)
                        pool.wait_ge(sem("xt_ready"), 2 * (2 * c + hh + 1))
                        for q in range(2):
                            nc.gpsimd.tensor_tensor(
                                Xl[:, 4 * q:4 * q + 4, :], Xt[:, 4 * q:4 * q + 4, :],
                                C(f"lev{lv}").unsqueeze(1).broadcast_to([P, 4, P]), ALU.mult).then_inc(sem("xl_ready"), 1)
            pool.wait_ge(sem("st_ready"), 9)
            pool.dma_start(out["p_wkv"], St).then_inc(sem("p_wkv_out"), 16)
            pool.wait_ge(sem("swkv_ready"), NH)
            pool.dma_start(out["s_wkv"], W("wkv")).then_inc(sem("s_wkv_out"), 16)
            pool.wait_ge(sem("p_wkv_out"), 16)
            pool.wait_ge(sem("ssm0_out"), 16)
            pool.wait_ge(sem("ssm1_out"), 16)
            pool.wait_ge(sem("s_wkv_out"), 16)
            pool.wait_ge(sem("shift_stored"), 16)
            pool.wait_ge(sem("l0_stored"), 16 * 7)

        @block.scalar
        def _(act):
            A = nc.scalar.activation
            n_act = [0]

            def link(ins):
                n_act[0] += 1
                ins.then_inc(sem("act_link"), 1)
                act.wait_ge(sem("act_link"), n_act[0])

            def squares(dst, src, need, name, n=KT):
                for k in range(n):
                    need(k)
                    A(dst[:, k, :], src[:, k, :], ACT.Square).then_inc(sem(name), 1)

            def root(g, dst, scale, eps):
                full(act, g)
                A(dst, bank(g)[:, 0:T], ACT.Sqrt, scale=scale, bias=eps).then_inc(freesem(g), 1)

            eps_cols = {}
            for n_, val in enumerate((EPS, HD * EPS, GN_EPS)):
                eps_cols[val] = vec[:, NVEC + 2 + n_:NVEC + 3 + n_]
            act.wait_ge(sem("eps_ready"), 1)
            act.wait_ge(sem("x_loaded"), 16)
            squares(sq0, x, lambda k: None, "sq_ready")
            root(base["N1"], rs[0], 1.0 / D, eps_cols[EPS])
            act.wait_ge(sem("cst_loaded"), 32)
            A(vec[0:16, NVEC + 1:NVEC + 2], v("alog", 0, 0, 16), ACT.Exp).then_inc(sem("aexp_ready"), 1)
            act.wait_ge(sem("h_ready"), 1)
            for t in range(KT):
                g = base["Z"] + t
                full(act, g)
                A(z[:, t, :], bank(g)[:, 0:T], ACT.Silu).then_inc(freesem(g), 1)

            def conv_out(t):
                act.wait_ge(sem("conv_done"), t + 1)
                A(xc[:, t, 0:TP], ctmp[t % 2][:, 0:TP], ACT.Silu)
                A(xc[:, t, TP:T].rearrange("p (b l) -> p b l", l=DL),
                  ctmp[t % 2][:, 3 + TP:padw].rearrange("p (b l) -> p b l", l=7)[:, :, 0:DL], ACT.Silu)\
                    .then_inc(sem("xc_ready"), 1)

            act.wait_ge(sem("pool_cleared"), 1)
            for t in range(CT):
                g = base["X"] + t
                full(act, g)
                if t >= 4:
                    act.wait_ge(sem("conv_done"), t - 3)
                    act.wait_ge(sem("tail_saved"), t - 3)
                A(pad[t % 4][:, 3:3 + TP], bank(g)[:, 0:TP], ACT.Copy).then_inc(sem("pad_half"), 1)
                act.wait_ge(sem("pad_half"), t + 1)
                A(pad[t % 4][:, 3 + TP:padw].rearrange("p (b n) -> p b n", n=7)[:, :, 3:7],
                  bank(g)[:, TP:T].rearrange("p (b l) -> p b l", l=DL), ACT.Copy).then_inc(freesem(g), 1)
                emptied(act, g)
                act.sem_inc(sem("pad_ready"), 1)
                if t >= 1:
                    conv_out(t - 1)
            conv_out(CT - 1)
            act.wait_ge(sem("dt_abs"), 1)
            A(dtt[2], dtt[1], ACT.Exp, scale=-1.0).then_inc(sem("dt_exp"), 1)
            for t in range(12):
                g = base["Q"] + t
                full(act, g)
                dst = qT[:, t, :] if t < 8 else kT[:, t - 8, :]
                A(dst, bank(g)[:, 0:T], ACT.Copy).then_inc(sem("qk_raw"), 1)
                A(qksq[:, t, :], bank(g)[:, 0:T], ACT.Square).then_inc(freesem(g), 1)
            for c, (t0, n) in enumerate(TOK):
                g = base["V"] + c
                full(act, g)
                A(vtok[0:n, c, :], bank(g)[0:n, 0:256], ACT.Copy).then_inc(freesem(g), 1)
            act.wait_ge(sem("wend_arg"), 1)
            A(dtt[5], dtt[4], ACT.Exp).then_inc(sem("wend_exp"), 1)
            for t in range(12):
                if 2 <= t < 10:
                    act.wait_ge(sem("q_normed"), t - 1)
                elif t >= 10:
                    act.wait_ge(sem("k_normed"), t - 9)
                root(base["QN"] + t, rs[t % 2], 1.0, eps_cols[HD * EPS])
            g = base["TT"]
            full(act, g)
            tmv = bank(g)[:, 0:288].rearrange("p (c n) -> p c n", c=3)
            link(A(TM[:, 0:2, :], tmv[:, 0:2, :], ACT.Copy))
            A(TM[0:TS, 2, :], tmv[0:TS, 2, :], ACT.Copy).then_inc(freesem(g), 1)
            g = base["BT"]
            full(act, g)
            A(Btok[:, 0:2, :], bank(g)[:, :].rearrange("p (c n) -> p c n", c=2), ACT.Copy).then_inc(freesem(g), 1)
            full(act, g + 1)
            A(Btok[0:TS, 2, :], bank(g + 1)[0:TS, 0:256], ACT.Copy).then_inc(freesem(g + 1), 1)
            for gg in range(2):
                g = base["H1"] + gg
                full(act, g)
                A(H1T[:, gg * 512:(gg + 1) * 512], bank(g), ACT.Copy).then_inc(freesem(g), 1)
            g = base["ES"]
            full(act, g)
            A(abq[0], bank(g), ACT.Copy).then_inc(sem("ab_ready"), 1)
            A(expq[0], bank(g), ACT.Exp).then_inc(freesem(g), 1)
            act.wait_ge(sem("e_arg"), 1)
            A(Eb[0][0:TS, :], Eb[0][0:TS, :], ACT.Exp).then_inc(sem("e_exp"), 1)
            act.wait_ge(sem("es_done"), 1)
            for qd in range(4):
                for c in range(2):
                    n = 2 * qd + c
                    g = base[f"E{qd}"] + c
                    full(act, g)
                    if qd >= 1:
                        act.wait_ge(sem("e_arg"), 1 + n - 1)
                    if c == 1 and qd >= 2:
                        emptied(act, base[f"Y{qd - 2}"] + 1)
                    A(abq[n % 2], bank(g), ACT.Copy).then_inc(sem("ab_ready"), 1)
                    if c == 1:
                        A(expq[qd % 2], bank(g), ACT.Exp).then_inc(freesem(g), 1)
                    else:
                        act.wait_ge(sem("ab_ready"), 2 + n)
                        act.sem_inc(freesem(g), 1)
                    act.wait_ge(sem("e_arg"), 2 + n)
                    e = Eb[n % 4]
                    A(e, e, ACT.Exp).then_inc(sem("e_exp"), 1)
            emptied(act, base["FS"] + 15)
            emptied(act, base["FP"] + 1)
            squares(ysq, z, lambda k: act.wait_ge(sem("y_gated"), k + 1), "sq_ready")
            for gg in range(2):
                root(base["YN"] + gg, rs[gg], 1.0 / 512, eps_cols[EPS])
            for j in range(4):
                s = j % 2
                st = stats[:, 32 * s:32 * s + 32]
                act.wait_ge(sem("att_max"), j + 1)
                for n in range(8):
                    pv = PP[s][:, n * 128:(n + 1) * 128] if n < 4 else PP[s][:, 512 + (n - 4) * 256:768 + (n - 4) * 256]
                    A(pv, pv, ACT.Exp, bias=st[:, n:n + 1], accum_out=st[:, 8 + n:9 + n])
                A(st[:, 16:24], st[:, 16:24], ACT.Exp).then_inc(sem("att_exp"), 1)
                for u in range(3):
                    g = base[f"PT{j}"] + u
                    full(act, g)
                    if j >= 2 and u == 0:
                        emptied(act, base[f"O{j - 2}"] + 1)
                    A(PT[s][:, u * 512:(u + 1) * 512], bank(g), ACT.Copy).then_inc(freesem(g), 1)
                for u in range(2):
                    g = base[f"O{j}"] + u
                    full(act, g)
                    A(oT[:, 2 * j + u, 0:TP], bank(g)[:, 0:TP], ACT.Copy).then_inc(freesem(g), 1)
            g = base["SS"]
            for u in range(4):
                n = P if u < 2 else TS
                dst = (SA if u < 2 else SBn).rearrange("p (n r l) -> p n r l", r=2, l=DL)[:, :, u % 2, :]
                full(act, g + u)
                A(dst, bank(g + u)[0:n, 0:256].rearrange("p (n l) -> p n l", l=DL), ACT.Copy).then_inc(freesem(g + u), 1)
            act.wait_ge(sem("satt_max"), 1)
            for jj in range(4):
                A(PS[:, jj, :], PS[:, jj, :], ACT.Exp, bias=stats[:, jj:jj + 1], accum_out=stats[:, 4 + jj:5 + jj])
            A(stats[:, 8:12], stats[:, 0:4], ACT.Exp, bias=v("sinkrow")).then_inc(sem("satt_exp"), 1)
            g = base["PTS"]
            full(act, g)
            A(PTA, bank(g), ACT.Copy).then_inc(freesem(g), 1)
            full(act, g + 1)
            A(PTB, bank(g + 1)[0:TS, :], ACT.Copy).then_inc(freesem(g + 1), 1)
            squares(sq2, x, lambda k: emptied(act, base["WO"] + k), "sq_ready")
            root(base["N2"], rs[0], 1.0 / D, eps_cols[EPS])
            emptied(act, base["WO"] + 7)
            act.wait_ge(sem("l0_stored"), 16 * 7)

            def ffn_heads(c, part):
                if part == "gu":
                    loaded(act, f"ffn{c}")
                else:
                    act.wait_ge(sem(f"ffn_down_loaded{c % RING}"), 16 * (c // RING + 1))
                if c >= 2:
                    full(act, base[f"FU{c - 2}"] + 3 if part == "gu" else base[f"FD{c - 2}"] + 7)
                for o in range(0, GU, 2048) if part == "gu" else (GU,):
                    A(mhead_[:, (c % 2) * SLOT + o:(c % 2) * SLOT + o + 2048], W(f"ffn{c}")[:, o:o + 2048], ACT.Copy)\
                        .then_inc(sem(f"ffn_{part}_head"), 1)

            ffn_heads(0, "gu")
            for k in range(KT):
                act.wait_ge(sem("h2_tile"), k + 1)
                A(hsplit[0][:, k, :], h[:, k, :], ACT.Copy).then_inc(sem("h_head"), 1)
            for c in range(FC):
                if c + 1 < FC:
                    ffn_heads(c + 1, "gu")
                ffn_heads(c, "dn")
                for u in range(2):
                    g = base[f"FU{c}"] + 2 * u
                    n = 2 * c + u
                    full(act, g)
                    if n >= 2:
                        act.wait_ge(sem("prod_ready"), n - 1)
                    A(sg[u], bank(g)[:, 0:T], ACT.Silu).then_inc(freesem(g), 1)
                for u in range(2):
                    n = 2 * c + u
                    act.wait_ge(sem("prod_ready"), n + 1)
                    if n >= 4:
                        full(act, base[f"FD{(n - 4) // 2}"] + 7)
                    A(actT[n % 4][0], prod[n % 4], ACT.Copy).then_inc(sem("act_head"), 1)
            squares(sq3, x, lambda k: emptied(act, base[f"FD{FC - 1}"] + k), "sq_ready")
            root(base["N3"], rs[0], 1.0 / D, eps_cols[EPS])
            for nm, dst in (("r", rT), ("k", k1), ("v", vT)):
                for t in range(KT):
                    g = base["R" + nm] + t
                    full(act, g)
                    A(dst[:, t, :], bank(g)[:, 0:T], ACT.Copy).then_inc(freesem(g), 1)
            for nm, fn, dst, bias in (("w", ACT.Tanh, sw, "w0"), ("a", ACT.Copy, aT, "a0"), ("g", ACT.Sigmoid, gT, None)):
                g = base["H" + nm]
                rows = 128 if nm == "g" else 64
                full(act, g)
                if nm == "g":
                    emptied(act, base["Rw"] + 7)
                A(hid["wag".index(nm) % 2][0:rows, :], bank(g)[0:rows, 0:T], fn).then_inc(freesem(g), 1)
                for t in range(KT):
                    g = base["R" + nm] + t
                    full(act, g)
                    if bias:
                        A(dst[:, t, :], bank(g)[:, 0:T], ACT.Sigmoid, bias=v(bias, t)).then_inc(freesem(g), 1)
                    else:
                        A(dst[:, t, :], bank(g)[:, 0:T], ACT.Copy).then_inc(freesem(g), 1)
            for t in range(KT):
                act.wait_ge(sem("kk_raw"), t + 1)
                if t >= 2:
                    emptied(act, base["KN"] + t - 2)
                A(tm1[t % 2], h[:, t, :], ACT.Square).then_inc(sem("kksq_ready"), 1)
                if t >= 1:
                    if t >= 3:
                        act.wait_ge(sem("kk_normed"), t - 2)
                    root(base["KN"] + t - 1, rs[(t - 1) % 2], 1.0, 0.0)
            act.wait_ge(sem("kk_normed"), KT - 2)
            root(base["KN"] + KT - 1, rs[(KT - 1) % 2], 1.0, 0.0)
            for t in range(KT):
                act.wait_ge(sem("cum_ready"), t + 1)
                A(AR[:, t, 1, :], xx[:, t, :], ACT.Exp, scale=-C_DECAY)
                A(AR[:, t, 0, :], sw[:, t, :], ACT.Exp, scale=-C_DECAY).then_inc(sem("decay_ready"), 1)
            act.wait_ge(sem("decay_ready"), KT)
            for t in range(KT):
                A(sw[:, t, :], xx[:, t, :], ACT.Exp, scale=C_DECAY).then_inc(sem("pinv_ready"), 1)
            def out_of(g, dst, src, fn=ACT.Copy):
                full(act, g)
                A(dst, src, fn).then_inc(freesem(g), 1)

            dve_done_aT = KT
            act.wait_ge(sem("tilde_ready"), dve_done_aT)
            act.wait_ge(sem("pinv_ready"), KT)
            for c in range(2):
                if c:
                    full(act, base["q011"] + 3)
                for n, dst in enumerate((v1, v1, b1, b1, k1t, k1t)):
                    g = base[f"VT{c}"] + n
                    out_of(g, dst[:, (n % 2) * 512:(n % 2 + 1) * 512], bank(g))
                for hh in range(2):
                    for lv in range(1, 6):
                        for q in range(2):
                            g = base[f"LY{c}{hh}{lv}"] + q
                            out_of(g, Yi[:, 4 * q:4 * q + 4, :], bank(g).rearrange("p (h t) -> p h t", t=P))
                    for cc in range(2):
                        g = base[f"q{c}{hh}{cc}"]
                        tb = 64 * cc
                        out_of(g, Zs[tb:tb + 64, :], bank(g)[tb:tb + 64, :])
                        out_of(g + 1, Us[tb:tb + 64, :], bank(g + 1)[tb:tb + 64, :])
                        tk = 128 * c + tb
                        out_of(g + 2, yT[:, 4 * hh:4 * hh + 4, tk:tk + 64], bank(g + 2)[:, 0:256].rearrange("p (k t) -> p k t", t=64))
            full(act, base["q111"] + 3)
            for n in range(6):
                g = base["sVT"] + n
                o = slice((n % 2) * 512, (n % 2 + 1) * 512)
                full(act, g)
                if n < 2:
                    A(v1[0:TS, o], bank(g)[0:TS, :], ACT.Copy)
                    A(UV[TS:64, o], bank(g)[0:TS, :], ACT.Copy).then_inc(freesem(g), 1)
                else:
                    r = 0 if n < 4 else TS
                    A(BK[r:r + TS, o], bank(g)[0:TS, :], ACT.Copy).then_inc(freesem(g), 1)
            g = base["sL"]
            out_of(g, Yi2, bank(g)[0:TS, :].rearrange("p (h t) -> p h t", t=TS))
            g = base["sZY"]
            full(act, g)
            zy = bank(g).rearrange("p (n a l) -> p n a l", a=2, l=DL)
            A(z1T.rearrange("p k (b l) -> p (k b) l", l=DL), zy[:, :, 0, :], ACT.Copy)
            A(y1.rearrange("p k (b l) -> p (k b) l", l=DL), zy[:, :, 1, :], ACT.Copy).then_inc(freesem(g), 1)
            for hh in range(2):
                g = base["sZ"] + hh
                out_of(g, Zs2[:, hh * 512:(hh + 1) * 512], bank(g)[0:TS, :])
            for hh in range(2):
                g = base["sU"] + hh
                out_of(g, UV[0:TS, hh * 512:(hh + 1) * 512], bank(g)[0:TS, :])
            for t in range(KT):
                act.wait_ge(sem("y_centred"), t + 1)
                if t >= 2:
                    emptied(act, base["GV"] + t - 2)
                A(tm1[t % 2], yT[:, t, :], ACT.Square).then_inc(sem("ysq_ready"), 1)
                if t >= 1:
                    if t >= 3:
                        act.wait_ge(sem("yg_ready"), t - 2)
                    root(base["GV"] + t - 1, rs[(t - 1) % 2], 1.0 / HD, eps_cols[GN_EPS])
            act.wait_ge(sem("yg_ready"), KT - 2)
            root(base["GV"] + KT - 1, rs[(KT - 1) % 2], 1.0 / HD, eps_cols[GN_EPS])
            squares(xi[0], x, lambda k: emptied(act, base["WR"] + k), "sq_ready")
            root(base["N4"], rs[0], 1.0 / D, eps_cols[EPS])
            emptied(act, base["WR"] + 7)
            for n in range(6):
                c, hf = divmod(n, 2)
                g = base["HT"] + n
                full(act, g)
                A(htok[0:TOK[c][1], c, hf * 512:(hf + 1) * 512], bank(g)[0:TOK[c][1], :], ACT.Copy).then_inc(freesem(g), 1)
            act.wait_ge(sem("gate_arg"), 1)
            A(gt[:, 0:2, 1:2], gt[:, 0:2, 0:1], ACT.Exp)
            A(gt[0:TS, 2, 1:2], gt[0:TS, 2, 0:1], ACT.Exp).then_inc(sem("gate_exp"), 1)
            act.wait_ge(sem("jobs_ready"), 1)
            njobs = act.value_load(jobi[0:1, 4:5], min_val=NE, max_val=NJ)

            def heads(j, c, part, pieces):
                s = c % MS
                act.wait_ge(sem(f"{part}_loaded{s}"), 16 * (uses[s] * j + c // MS + 1))
                if part == "dn" and c >= 2:
                    act.wait_ge(sem(f"dn_slot_free{(c - 2) % MS}"), uses[(c - 2) % MS] * j + (c - 2) // MS + 2)
                for i in pieces:
                    o = i * 2048 + (GU if part == "dn" else 0)
                    A(mhead[c % 2][:, o:o + 2048], mslot[s][:, o:o + 2048], ACT.Copy).then_inc(sem(f"{part}_head"), 1)

            with act.Fori(0, njobs) as j:
                heads(j, 0, "gu", range(2))
                for u in range(2):
                    act.wait_ge(sem("gather_full"), 3 * j + 1 + u)
                    A(hsel[0][:, 4 * u:4 * u + 4, :], ps[:, 5 + u, :].rearrange("p (k c) -> p k c", k=4), ACT.Copy)\
                        .then_inc(sem("hsel_head"), 1)
                act.wait_ge(sem("gather_full"), 3 * j + 3)
                A(Wt, ps[:, 7, 0:T], ACT.Copy).then_inc(sem("wt_ready"), 1)
                heads(j, 1, "gu", range(2))
                for c in range(FC + 1):
                    if c < FC:
                        act.wait_ge(sem("gu_full"), FC * j + c + 1)
                        act.sem_inc(sem(f"gu_slot_free{c % MS}"), 1)
                        act.wait_ge(sem("gu_free"), FC * j + c + 2)
                        A(sgm, ps[:, c % 2, 0:256], ACT.Silu).then_inc(sem("silu_ready"), 1)
                    if c + 2 < FC:
                        heads(j, c + 2, "gu", range(0, 1))
                    if c:
                        act.wait_ge(sem("tr_full"), FC * j + c)
                        A(actTm[(c - 1) % 2][0], ps[:, 2, 0:256], ACT.Copy).then_inc(sem("tr_head"), 1)
                    if c + 2 < FC:
                        heads(j, c + 2, "gu", range(1, 2))
                    if c < FC:
                        heads(j, c, "dn", range(1))
                act.wait_ge(sem(f"dn_slot_free{(FC - 1) % MS}"), uses[(FC - 1) % MS] * (j + 1) + 1)
                act.wait_ge(sem("scattered"), KT * j + 1)
                A(ysb[:, 0:512], ps[:, 3, :], ACT.Copy)
                A(ysb[:, 512:1024], ps[:, 4, :], ACT.Copy).then_inc(sem("y_out"), 1)

        @block.vector
        def _(dve):
            V = nc.vector
            n_dve = [0]

            def link(ins):
                n_dve[0] += 1
                ins.then_inc(sem("dve_link"), 1)
                dve.wait_ge(sem("dve_link"), n_dve[0])

            def norm(g, wname, signal, n, tile_signal=None):
                emptied(dve, g)
                link(V.reciprocal(rs[0], rs[0]))
                for k in range(KT):
                    last = V.scalar_tensor_tensor(h[:, k, :], x[:, k, :], v(wname, k), rs[0], ALU.mult, ALU.mult)
                    if tile_signal:
                        last.then_inc(sem(tile_signal), 1)
                if tile_signal:
                    return
                last.then_inc(sem(signal), 1)
                dve.wait_ge(sem(signal), n)

            dve.wait_ge(sem("cst_loaded"), 32)
            dve.wait_ge(sem("x_loaded"), 16)
            V.tensor_scalar(kn8, v("kn"), 8.0, None, ALU.mult)
            norm(base["N1"], "nm0", "h_ready", 1)
            for t in range(CT):
                dve.wait_ge(sem("pad_ready"), t + 1)
                dve.wait_ge(sem("padstate_ready"), t + 1)
                if t >= 2:
                    dve.wait_ge(sem("xc_ready"), t - 1)
                pd, ct = pad[t % 4], ctmp[t % 2]
                n = padw - 3
                link(V.tensor_scalar(ct[:, 0:n], pd[:, 0:n], v("convw", 4 * t), v("convb", t), ALU.mult, ALU.add))
                for j in range(1, 4):
                    ins = V.scalar_tensor_tensor(ct[:, 0:n], pd[:, j:j + n], v("convw", 4 * t + j), ct[:, 0:n], ALU.mult, ALU.add)
                    if j < 3:
                        link(ins)
                ins.then_inc(sem("conv_done"), 1)
            g = base["DT"]
            full(dve, g)
            dve.wait_ge(sem("aexp_ready"), 1)
            V.tensor_scalar(dtt[0], bank(g)[0:16, 0:T], v("dtb", 0, 0, 16), None, ALU.add).then_inc(freesem(g), 1)
            emptied(dve, g)
            V.scalar_tensor_tensor(dtt[1], dtt[0], -1.0, dtt[0], ALU.mult, ALU.max).then_inc(sem("dt_abs"), 1)
            dve.wait_ge(sem("dt_exp"), 1)
            link(V.tensor_scalar(dtt[3], dtt[2], 2.0, None, ALU.add))
            link(V.reciprocal(dtt[3], dtt[3]))
            link(V.tensor_tensor(dtt[2], dtt[2], dtt[3], ALU.mult))
            link(V.tensor_tensor(dtt[3], dtt[2], dtt[2], ALU.mult))
            link(V.tensor_scalar(dtt[1], dtt[3], 1.0 / 15, None, ALU.mult))
            for c in (13, 11, 9, 7, 5, 3):
                link(V.scalar_tensor_tensor(dtt[1], dtt[1], 1.0 / c, dtt[3], ALU.add, ALU.mult))
            link(V.scalar_tensor_tensor(dtt[1], dtt[1], 1.0, dtt[2], ALU.add, ALU.mult))
            link(V.tensor_scalar(dtt[0], dtt[0], 0.0, None, ALU.max))
            dve.wait_ge(sem("pool_cleared"), 1)
            link(V.scalar_tensor_tensor(SC[0:16, :], dtt[1], 2.0, dtt[0], ALU.mult, ALU.add))
            link(V.tensor_scalar(dtt[3], SC[0:16, :], vec[0:16, NVEC + 1:NVEC + 2], -1.0, ALU.mult, ALU.mult))
            link(V.tensor_tensor_scan(acs[0:16, :], C("reset128", 16), dtt[3], 0.0, ALU.mult, ALU.add))
            for c in range(2):
                o = c * 128
                V.tensor_scalar(dtt[4][:, o:o + 128], acs[0:16, o:o + 128], acs[0:16, o + 127:o + 128], -1.0,
                                ALU.subtract, ALU.mult)
            asm = acs[0:16, TP:T].rearrange("p (b l) -> p b l", l=DL)
            V.tensor_copy(SC[32:48, :], acs[0:16, :])
            V.tensor_tensor(dtt[4][:, TP:T].rearrange("p (b l) -> p b l", l=DL), asm[:, :, 3:4].broadcast_to([16, DB, DL]),
                            asm, ALU.subtract).then_inc(sem("wend_arg"), 1)
            dve.wait_ge(sem("wend_exp"), 1)
            V.tensor_tensor(SC[64:80, :], dtt[5], SC[0:16, :], ALU.mult).then_inc(sem("sc_ready"), 1)
            for t in range(12):
                g = base["QN"] + t
                emptied(dve, g)
                dve.wait_ge(sem("qk_raw"), t + 1)
                link(V.reciprocal(rs[t % 2], rs[t % 2]))
                if t < 8:
                    V.scalar_tensor_tensor(qT[:, t, :], qT[:, t, :], v("qn"), rs[t % 2], ALU.mult, ALU.mult)\
                        .then_inc(sem("q_normed"), 1)
                else:
                    V.scalar_tensor_tensor(kT[:, t - 8, :], kT[:, t - 8, :], kn8, rs[t % 2], ALU.mult, ALU.mult)\
                        .then_inc(sem("k_normed"), 1)
            emptied(dve, base["TT"])
            for c, (t0, n) in enumerate(TOK):
                for hf in range(2):
                    g = base["XT"] + 2 * c + hf
                    full(dve, g)
                    src = bank(g)[0:n, :].rearrange("p (h d) -> p h d", d=HD)
                    for dst, o in ((xdt, 0), (xdec, 64)):
                        ins = V.tensor_tensor(dst[0:n, c, hf * 512:(hf + 1) * 512].rearrange("p (h d) -> p h d", d=HD), src,
                                              TM[0:n, c, o + 8 * hf:o + 8 * hf + 8].unsqueeze(2).broadcast_to([n, 8, HD]), ALU.mult)
                    ins.then_inc(freesem(g), 1)
            g = base["CB"]
            full(dve, g)
            V.tensor_tensor(hb[:, 0:512].rearrange("p (c q) -> p c q", q=P), bank(g).rearrange("p (c q) -> p c q", q=P),
                            C("tri").unsqueeze(1).broadcast_to([P, 4, P]), ALU.mult).then_inc(freesem(g), 1)
            full(dve, g + 1)
            V.tensor_tensor(CBs, bank(g + 1)[0:TS, 0:64].rearrange("p (c q) -> p c q", q=TS),
                            C("tris", TS).unsqueeze(1).broadcast_to([TS, 2, TS]), ALU.mult).then_inc(freesem(g + 1), 1)
            dve.wait_ge(sem("ab_ready"), 1)
            e = Eb[0][0:TS, :].rearrange("p (h t) -> p h t", t=TS)
            link(V.tensor_tensor(e, abq[0][0:TS, :].rearrange("p (h t) -> p h t", t=TS),
                                 TM[0:TS, 2, 32:48].unsqueeze(2).broadcast_to([TS, NH, TS]), ALU.subtract))
            V.tensor_scalar(Eb[0][0:TS, :], Eb[0][0:TS, :], 0.0, None, ALU.min).then_inc(sem("e_arg"), 1)
            emptied(dve, base["ES"])
            eq = expq[0].rearrange("p (h t) -> p h t", t=TS)
            V.tensor_copy(dsm, expq[0].rearrange("p (h b l) -> p h b l", b=DB, l=DL)[:, :, :, 3])
            for g in range(2):
                V.tensor_tensor(CsS[:, 8 * g:8 * g + 8, :], eq[:, 8 * g:8 * g + 8, :],
                                xc[:, 10 + g, TP:T].unsqueeze(1).broadcast_to([P, 8, TS]), ALU.mult)
            dve.wait_ge(sem("e_exp"), 1)
            for g in range(2):
                ins = V.tensor_tensor(Ms[:, 8 * g:8 * g + 8, :], e[:, 8 * g:8 * g + 8, :],
                                      CBs[:, g, :].unsqueeze(1).broadcast_to([TS, 8, TS]), ALU.mult)
            ins.then_inc(sem("es_done"), 1)

            def y_gate(i):
                g = base[f"Y{i // 2}"] + i % 2
                full(dve, g)
                link(V.scalar_tensor_tensor(rs[0], xc[:, i, :], v("dskip", i), bank(g)[:, 0:T], ALU.mult, ALU.add))
                V.tensor_tensor(z[:, i, :], z[:, i, :], rs[0], ALU.mult).then_inc(freesem(g), 1)
                emptied(dve, g)
                dve.sem_inc(sem("y_gated"), 1)

            for qd in range(4):
                for c in range(2):
                    n = 2 * qd + c
                    dve.wait_ge(sem("ab_ready"), 2 + n)
                    if qd >= 2:
                        emptied(dve, base[f"Y{qd - 2}"] + 1)
                    e = Eb[n % 4]
                    for k in range(4):
                        ins = V.tensor_scalar(e[:, k * P:(k + 1) * P], abq[n % 2][:, k * P:(k + 1) * P],
                                              TM[:, c, 32 + 4 * qd + k:33 + 4 * qd + k], 0.0, ALU.subtract, ALU.min)
                    ins.then_inc(sem("e_arg"), 1)
                    dve.wait_ge(sem("e_exp"), 2 + n)
                    e3 = e.rearrange("p (h q) -> p h q", q=P)
                    gg = qd // 2
                    ins = V.tensor_tensor(e3, e3, CBm[:, c, gg, :].unsqueeze(1).broadcast_to([P, 4, P]), ALU.mult)
                    if c == 1:
                        emptied(dve, base[f"E{qd}"] + 1)
                        eq = expq[qd % 2].rearrange("p (h q) -> p h q", q=P)
                        link(V.tensor_copy(dend[:, 4 * qd:4 * qd + 4], eq[:, :, P - 1]))
                        ins = V.tensor_tensor(eq, eq, xc[:, 10 + gg, P:2 * P].unsqueeze(1).broadcast_to([P, 4, P]), ALU.mult)
                        ins.then_inc(sem("cs_ready"), 1)
                if qd >= 1:
                    y_gate(2 * qd - 2)
                    y_gate(2 * qd - 1)
            y_gate(6)
            y_gate(7)
            for gg in range(2):
                g = base["FP"] + gg
                hv = H1T[:, gg * 512:(gg + 1) * 512]
                hv3 = hv.rearrange("p (h c) -> p h c", c=HD)
                full(dve, g)
                link(V.tensor_tensor(hv3, hv3, dend[:, 8 * gg:8 * gg + 8].unsqueeze(2).broadcast_to([P, 8, HD]), ALU.mult))
                V.tensor_tensor(hv, hv, bank(g), ALU.add).then_inc(freesem(g), 1)
                emptied(dve, g)
                dve.sem_inc(sem("pssm_ready"), 1)
            for gg in range(2):
                for b in range(DB):
                    g = base["FS"] + gg * DB + b
                    full(dve, g)
                    dve.wait_ge(sem("ssm_decayed"), gg * DB + b + 1)
                    sv = W(f"ssm{gg}")[:, b * 512:(b + 1) * 512]
                    V.tensor_tensor(sv, sv, bank(g), ALU.add).then_inc(freesem(g), 1)
                    emptied(dve, g)
                    dve.sem_inc(sem("sssm_ready"), 1)
            for gg in range(2):
                g = base["YN"] + gg
                emptied(dve, g)
                link(V.reciprocal(rs[gg], rs[gg]))
                for i in range(4 * gg, 4 * gg + 4):
                    ins = V.scalar_tensor_tensor(z[:, i, :], z[:, i, :], v("ssdn", i), rs[gg], ALU.mult, ALU.mult)
            ins.then_inc(sem("yssd_ready"), 1)
            dve.wait_ge(sem("l0_loaded"), 32)

            def att_scores(j):
                s = j % 2
                g = base[f"S{j}"]
                st = stats[:, 32 * s:32 * s + 32]
                if j >= 2:
                    emptied(dve, base[f"PT{j - 2}"] + 2)
                p0 = PP[s][:, 0:512].rearrange("p (h k) -> p h k", k=128)
                for u in range(4):
                    nk = 128 * (u // 2 + 1)
                    area_ = PP[s][:, 0:512] if u < 2 else PP[s][:, 512:1536]
                    dst = area_.rearrange("p (n r k) -> p n r k", n=2, r=2)[:, :, u % 2, :]
                    mask = am[:, 0:128] if u < 2 else am[:, 128:384]
                    full(dve, g + u)
                    V.tensor_tensor(dst, bank(g + u)[:, 0:2 * nk].rearrange("p (n k) -> p n k", n=2),
                                    mask.unsqueeze(1).broadcast_to([P, 2, nk]), ALU.add).then_inc(freesem(g + u), 1)
                for u in range(4):
                    emptied(dve, g + u)
                V.reduce_max(st[:, 0:4], p0, AX)
                link(V.reduce_max(st[:, 4:8], PP[s][:, 512:1536].rearrange("p (h k) -> p h k", k=256), AX))
                o = VEC["sinks"][0]
                sk = vec[:, o + 4 * j:o + 4 * j + 4].unsqueeze(1).broadcast_to([P, 2, 4])
                s3 = st[:, 0:8].rearrange("p (a h) -> p a h", a=2)
                link(V.tensor_tensor(s3, s3, sk, ALU.max))
                V.tensor_tensor(st[:, 16:24].rearrange("p (a h) -> p a h", a=2), sk, s3, ALU.subtract)
                link(V.tensor_scalar(st[:, 24:32], st[:, 0:8], -1.0, None, ALU.mult))
                V.tensor_copy(st[:, 0:8], st[:, 24:32]).then_inc(sem("att_max"), 1)

            def att_probs(j):
                s = j % 2
                st = stats[:, 32 * s:32 * s + 32]
                dve.wait_ge(sem("att_exp"), j + 1)
                link(V.tensor_tensor(st[:, 8:16], st[:, 8:16], st[:, 16:24], ALU.add))
                link(V.reciprocal(st[:, 8:16], st[:, 8:16]))
                for n in range(8):
                    pv = PP[s][:, n * 128:(n + 1) * 128] if n < 4 else PP[s][:, 512 + (n - 4) * 256:768 + (n - 4) * 256]
                    ins = V.tensor_scalar(pv, pv, st[:, 8 + n:9 + n], None, ALU.mult)
                ins.then_inc(sem("p_ready"), 1)

            for j in range(4):
                att_scores(j)
                if j > 0:
                    att_probs(j - 1)
            att_probs(3)
            for u in range(2):
                g = base["ST"] + u
                full(dve, g)
                V.tensor_tensor(PS[:, 2 * u:2 * u + 2, :], bank(g)[:, 0:320].rearrange("p (j k) -> p j k", k=160),
                                am[:, 384 + u * 320:704 + u * 320].rearrange("p (j k) -> p j k", k=160), ALU.add)\
                    .then_inc(freesem(g), 1)
            emptied(dve, g - 1)
            emptied(dve, g)
            link(V.reduce_max(stats[:, 12:16], PS[:, :, :], AX))
            dve.wait_ge(sem("att_exp"), 4)
            V.tensor_scalar(stats[:, 0:4], stats[:, 12:16], v("sinkrow"), -1.0, ALU.max, ALU.mult).then_inc(sem("satt_max"), 1)
            dve.wait_ge(sem("satt_exp"), 1)
            link(V.tensor_tensor(stats[:, 4:8], stats[:, 4:8], stats[:, 8:12], ALU.add))
            link(V.reciprocal(stats[:, 4:8], stats[:, 4:8]))
            V.tensor_tensor(PS[:, :, :], PS[:, :, :], stats[:, 4:8].unsqueeze(2).broadcast_to([P, 4, 160]), ALU.mult)\
                .then_inc(sem("ps_ready"), 1)
            g = base["OS"]
            osv = oT[:, :, TP:T]
            full(dve, g)
            V.tensor_copy(osv, bank(g)[:, 0:256].rearrange("p (i t) -> p i t", t=TS)).then_inc(freesem(g), 1)
            full(dve, g + 1)
            emptied(dve, g)
            V.tensor_tensor(osv, osv, bank(g + 1)[:, 0:256].rearrange("p (i t) -> p i t", t=TS), ALU.add)\
                .then_inc(freesem(g + 1), 1)

            def residual(g, m):
                full(dve, g)
                V.tensor_tensor(x[:, m, :], x[:, m, :], bank(g)[:, 0:T], ALU.add).then_inc(freesem(g), 1)

            for m in range(KT):
                residual(base["WO"] + m, m)
            emptied(dve, base["WO"] + 7)
            dve.wait_ge(sem("l0_stored"), 16 * 7)
            norm(base["N2"], "nf0", None, 0, "h2_tile")

            def ffn_rests(c, part):
                n = 2 if part == "gu" else 1
                o0 = (where[f"ffn{c}"] % RING) * SLOT
                for i, o in enumerate(range(0, GU, 2048) if part == "gu" else (GU,)):
                    dve.wait_ge(sem(f"ffn_{part}_head"), n * c + i + 1)
                    V.tensor_tensor(rest_ring[:, o0 + o:o0 + o + 2048], ring[:, o0 + o:o0 + o + 2048],
                                    mhead_[:, (c % 2) * SLOT + o:(c % 2) * SLOT + o + 2048].bitcast(F32), ALU.subtract)\
                        .then_inc(sem(f"ffn_{part}_split"), 1)

            ffn_rests(0, "gu")
            for k in range(KT):
                dve.wait_ge(sem("h_head"), k + 1)
                V.tensor_tensor(hsplit[1][:, k, :], h[:, k, :], hsplit[0][:, k, :].bitcast(F32), ALU.subtract)\
                    .then_inc(sem("h_split"), 1)
            for c in range(FC + 1):
                if c + 1 < FC:
                    ffn_rests(c + 1, "gu")
                if c < FC:
                    ffn_rests(c, "dn")
                for u in range(2):
                    if c == FC:
                        break
                    g = base[f"FU{c}"] + 2 * u + 1
                    n = 2 * c + u
                    full(dve, g)
                    emptied(dve, g - 1)
                    V.tensor_tensor(prod[n % 4], sg[u], bank(g)[:, 0:T], ALU.mult).then_inc(freesem(g), 1)
                    emptied(dve, g)
                    dve.sem_inc(sem("prod_ready"), 1)
                for u in range(2):
                    if c == FC:
                        break
                    n = 2 * c + u
                    dve.wait_ge(sem("act_head"), n + 1)
                    V.tensor_tensor(actT[n % 4][1], prod[n % 4], actT[n % 4][0].bitcast(F32), ALU.subtract)\
                        .then_inc(sem("act_split"), 1)
                for m in range(KT):
                    if c:
                        if c > 1:
                            emptied(dve, base[f"FD{c - 2}"] + m)
                        residual(base[f"FD{c - 1}"] + m, m)
            emptied(dve, base[f"FD{FC - 1}"] + 7)
            norm(base["N3"], "nm1", "h_ready", 2)
            dve.wait_ge(sem("shift_loaded"), 16)
            V.tensor_copy(shiftout[:, :, 0], h[:, :, TP - 1]).then_inc(sem("shiftout_ready"), 1)
            hs = h[:, :, TP:T].rearrange("p k (b l) -> p k b l", l=DL)
            xs = xx[:, :, TP:T].rearrange("p k (b l) -> p k b l", l=DL)
            V.tensor_copy(shiftout[:, :, 1:9], hs[:, :, :, 3]).then_inc(sem("shiftout_ready"), 1)
            V.tensor_tensor(xx[:, :, 1:TP], h[:, :, 0:TP - 1], h[:, :, 1:TP], ALU.subtract)
            V.tensor_scalar(xx[:, :, 0], h[:, :, 0], -1.0, None, ALU.mult)
            for k in range(KT):
                V.tensor_tensor(xs[:, k, :, 1:DL], hs[:, k, :, 0:DL - 1], hs[:, k, :, 1:DL], ALU.subtract)
            link(V.tensor_tensor(xs[:, :, :, 0], shiftst, hs[:, :, :, 0], ALU.subtract))
            users = [base["Rr"] + 7, base["Rk"] + 7, base["Rv"] + 7, base["Hw"], base["Ha"], base["Hg"]]
            for n, mrow in enumerate((0, 2, 3, 1, 4, 5)):
                if n >= 2:
                    full(dve, users[n - 2])
                for k in range(KT):
                    V.scalar_tensor_tensor(xi[n % 2][:, k, :], xx[:, k, :], v("mu", 8 * mrow + k), h[:, k, :],
                                           ALU.mult, ALU.add).then_inc(sem("xi_ready"), 1)
            o = VEC["ka"][0]
            link(V.tensor_scalar(omka, vec[:, o:o + 8], -1.0, 1.0, ALU.mult, ALU.add))
            full(dve, users[5])
            dve.wait_ge(sem("xi_ready"), 48)
            for t in range(KT):
                emptied(dve, base["Rw"] + t)
                link(V.tensor_tensor_scan(xx[:, t, :], C("reset64"), sw[:, t, :], 0.0, ALU.mult, ALU.add))
                V.tensor_tensor(sw[:, t, :], xx[:, t, :], sw[:, t, :], ALU.subtract).then_inc(sem("cum_ready"), 1)
            for t in range(KT):
                emptied(dve, base["Rk"] + t)
                V.tensor_scalar(h[:, t, :], k1[:, t, :], v("kk", t), None, ALU.mult).then_inc(sem("kk_raw"), 1)
            for t in range(KT):
                g = base["KN"] + t
                emptied(dve, g)
                link(V.tensor_scalar(rs[t % 2], rs[t % 2], 1e-12, None, ALU.max))
                link(V.reciprocal(rs[t % 2], rs[t % 2]))
                V.tensor_tensor(h[:, t, :], h[:, t, :], rs[t % 2], ALU.mult).then_inc(sem("kk_normed"), 1)
            for t in range(KT):
                emptied(dve, base["Ra"] + t)
                dve.wait_ge(sem("kk_normed"), KT)
                link(V.tensor_scalar(rs[0], aT[:, t, :], v("ka", t), omka[:, t:t + 1], ALU.mult, ALU.add))
                link(V.tensor_tensor(k1[:, t, :], k1[:, t, :], rs[0], ALU.mult))
                if t >= 2:
                    full(dve, base["BO"] + t - 2)
                V.scalar_tensor_tensor(tm1[t % 2], rT[:, t, :], v("rk", t), k1[:, t, :], ALU.mult, ALU.mult)\
                    .then_inc(sem("bonus_ready"), 1)
                dve.wait_ge(sem("decay_ready"), t + 1)
                V.tensor_copy(Pend[:, t, 0:4], AR[:, t, 1, 63:TP:64])
                link(V.tensor_copy(Pend[:, t, 4:12], AR[:, t, 1, TP + 3:T:DL]))
                V.tensor_tensor(AR[:, t, 1, :], AR[:, t, 1, :], rT[:, t, :], ALU.mult)
                V.scalar_tensor_tensor(AR[:, t, 0, :], AR[:, t, 0, :], -1.0, h[:, t, :], ALU.mult, ALU.mult)
                link(V.tensor_tensor(aT[:, t, :], aT[:, t, :], h[:, t, :], ALU.mult))
                if t >= 1:
                    bonus_out = base["BO"] + t - 1
                    full(dve, bonus_out)
                    V.tensor_tensor(rT[:, t - 1, :], vT[:, t - 1, :], bank(bonus_out)[:, 0:T], ALU.mult)\
                        .then_inc(freesem(bonus_out), 1)
            full(dve, base["BO"] + 7)
            V.tensor_tensor(rT[:, 7, :], vT[:, 7, :], bank(base["BO"] + 7)[:, 0:T], ALU.mult).then_inc(freesem(base["BO"] + 7), 1)
            for t in range(KT):
                dve.wait_ge(sem("pinv_ready"), t + 1)
                V.tensor_tensor(aT[:, t, :], aT[:, t, :], sw[:, t, :], ALU.mult)
                V.tensor_tensor(k1[:, t, :], k1[:, t, :], sw[:, t, :], ALU.mult).then_inc(sem("tilde_ready"), 1)
            dve.wait_ge(sem("tilde_ready"), KT)
            V.memset(scr[:, 5120:6144], 0.0).then_inc(sem("st_ready"), 1)
            dve.wait_ge(sem("st_ready"), 1)
            idb = ident.unsqueeze(1).broadcast_to([P, 4, P])
            for c in range(2):
                for hh in range(2):
                    idx = 2 * c + hh
                    if idx:
                        full(dve, base[f"q{(idx - 1) // 2}{(idx - 1) % 2}1"] + 3)
                    for n in range(8):
                        g = base[f"A{c}{hh}"] + n
                        full(dve, g)
                        V.tensor_tensor(A4f[:, n * 512:(n + 1) * 512], bank(g), C("m4"), ALU.mult).then_inc(freesem(g), 1)
                    for q in range(2):
                        g = base[f"X{c}{hh}"] + q
                        qs = slice(4 * q, 4 * q + 4)
                        full(dve, g)
                        if idx:
                            dve.wait_ge(sem("xl_ready"), 10 * idx)
                        V.tensor_tensor(Xt[:, q:8:2, :], bank(g).rearrange("p (h t) -> p h t", t=P),
                                        C("low").unsqueeze(1).broadcast_to([P, 4, P]), ALU.mult).then_inc(freesem(g), 1)
                        emptied(dve, g)
                        dve.sem_inc(sem("xt_ready"), 1)
                    emptied(dve, base[f"A{c}{hh}"] + 7)
                    for q in range(2):
                        qs = slice(4 * q, 4 * q + 4)
                        V.tensor_tensor(Mi[:, qs, :], A4[:, qs, 0, :], C("lev0u").unsqueeze(1).broadcast_to([P, 4, P]), ALU.mult)
                        link(V.tensor_tensor(Mti[:, qs, :], Xt[:, qs, :], C("lev0").unsqueeze(1).broadcast_to([P, 4, P]), ALU.mult))
                        V.tensor_tensor(Mi[:, qs, :], Mi[:, qs, :], idb, ALU.add)
                        V.tensor_tensor(Mti[:, qs, :], Mti[:, qs, :], idb, ALU.add).then_inc(sem("m0_ready"), 1)
                    dve.wait_ge(sem("m0_ready"), 2 * idx + 2)
                    for lv in range(1, 6):
                        for nm, dst in (("LM", Mi), ("LT", Mti)):
                            if nm == "LT" and lv == 5:
                                continue
                            for q in range(2):
                                g = base[f"{nm}{c}{hh}{lv}"] + q
                                qs = slice(4 * q, 4 * q + 4)
                                if lv > 1:
                                    emptied(dve, base[f"{nm}{c}{hh}{lv - 1}"] + q)
                                full(dve, g)
                                V.tensor_tensor(dst[:, qs, :], dst[:, qs, :], bank(g).rearrange("p (h t) -> p h t", t=P),
                                                ALU.add).then_inc(freesem(g), 1)
                    for cc in range(2):
                        g = base[f"q{c}{hh}{cc}"] + 3
                        full(dve, g)
                        ks = slice(4 * hh, 4 * hh + 4)
                        new = St[:, 256 * hh:256 * hh + 256].rearrange("p (k v) -> p k v", v=HD)
                        pv = bank(g)[:, 0:256].rearrange("p (k v) -> p k v", v=HD)
                        for par in range(2):
                            pr = slice(64 * par, 64 * par + 64)
                            ins = V.tensor_tensor(new[pr], Sd[pr, ks, par, :], pv[pr], ALU.add)
                        ins.then_inc(freesem(g), 1)
                        emptied(dve, g)
                        for par in range(2):
                            pr = slice(64 * par, 64 * par + 64)
                            dst = new[pr] if c and cc else Sd[pr, ks, par, :]
                            ins = V.tensor_tensor(dst, new[pr], Pend[pr, ks, 2 * c + cc].unsqueeze(2).broadcast_to([64, 4, HD]),
                                                  ALU.mult)
                        ins.then_inc(sem("st_ready"), 1)
                        dve.wait_ge(sem("st_ready"), 4 * c + 2 * hh + cc + 2)
            full(dve, base["q111"] + 3)
            for n in range(4):
                g = base["sA"] + n
                full(dve, g)
                V.tensor_tensor(A4f[0:TS, 0:2048].rearrange("p (i r m) -> p i r m", i=8, r=2)[:, 4 * (n // 2):4 * (n // 2) + 4, n % 2, :],
                                bank(g)[0:TS, :].rearrange("p (h m) -> p h m", h=4),
                                C("m4s", TS).unsqueeze(1).broadcast_to([TS, 4, 4 * TS]), ALU.mult).then_inc(freesem(g), 1)
            def bc16(name):
                return C(name)[0:TS, 0:TS].unsqueeze(1).broadcast_to([TS, NH, TS])

            for par in range(2):
                g = base["sX"] + par
                full(dve, g)
                V.tensor_tensor(Xt2[:, par:NH:2, :], bank(g)[0:TS, 0:256].rearrange("p (h t) -> p h t", t=TS),
                                C("lows", TS).unsqueeze(1).broadcast_to([TS, 8, TS]), ALU.mult).then_inc(freesem(g), 1)
                emptied(dve, g)
            emptied(dve, base["sA"] + 3)
            dve.wait_ge(sem("xl_ready"), 40)
            V.tensor_tensor(M2, A4s[:, :, 0, :], bc16("lev0u"), ALU.mult)
            V.tensor_tensor(Xl2, Xt2, bc16("lev1"), ALU.mult)
            link(V.tensor_tensor(Mt2, Xt2, bc16("lev0"), ALU.mult))
            V.tensor_tensor(M2, M2, bc16("ident"), ALU.add)
            V.tensor_tensor(Mt2, Mt2, bc16("ident"), ALU.add).then_inc(sem("m2_ready"), 1)
            dve.wait_ge(sem("m2_ready"), 1)
            g = base["sL"] + 1
            full(dve, g)
            V.tensor_tensor(M2, M2, bank(g)[0:TS, :].rearrange("p (h t) -> p h t", t=TS), ALU.add).then_inc(freesem(g), 1)
            emptied(dve, base["sU"] + 1)
            wk = W("wkv").rearrange("p (k b v) -> p k b v", k=KT, b=DB)
            bmk = C("bmask", 64).unsqueeze(2).broadcast_to([64, DB, HD])

            def uv_masked(hd):
                if hd >= 2:
                    full(dve, base["sS"] + hd - 2)
                V.tensor_tensor(UVm[hd % 2], UV[:, hd * HD:(hd + 1) * HD].unsqueeze(1).broadcast_to([64, DB, HD]), bmk, ALU.mult)\
                    .then_inc(sem("uvm_ready"), 1)

            uv_masked(0)
            for hd in range(NH):
                if hd + 1 < NH:
                    uv_masked(hd + 1)
                g = base["sS"] + hd
                r0 = 64 * (hd % 2)
                full(dve, g)
                sv = wk[r0:r0 + 64, hd // 2]
                V.tensor_tensor(sv, sv, bank(g)[r0:r0 + 64, :].rearrange("p (b v) -> p b v", b=DB), ALU.add).then_inc(freesem(g), 1)
                emptied(dve, g)
                V.tensor_tensor(sv, sv, Pend[r0:r0 + 64, hd // 2, 4:12].unsqueeze(2).broadcast_to([64, DB, HD]), ALU.mult)\
                    .then_inc(sem("swkv_ready"), 1)
            g = base["sY"]
            full(dve, g)
            V.tensor_tensor(yT[:, :, TP:T], bank(g)[:, 0:256].rearrange("p (k t) -> p k t", t=TS), y1, ALU.add)\
                .then_inc(freesem(g), 1)
            emptied(dve, g)
            emptied(dve, base["q111"] + 2)
            for t in range(KT):
                g = base["GM"] + t
                full(dve, g)
                V.scalar_tensor_tensor(yT[:, t, :], bank(g)[:, 0:T], -1.0 / HD, yT[:, t, :], ALU.mult, ALU.add)\
                    .then_inc(freesem(g), 1)
                emptied(dve, g)
                dve.sem_inc(sem("y_centred"), 1)
            for t in range(KT):
                g = base["GV"] + t
                emptied(dve, g)
                link(V.reciprocal(rs[t % 2], rs[t % 2]))
                link(V.tensor_tensor(yT[:, t, :], rs[t % 2], yT[:, t, :], ALU.mult))
                link(V.tensor_scalar(yT[:, t, :], yT[:, t, :], v("lnw", t), v("lnb", t), ALU.mult, ALU.add))
                link(V.tensor_tensor(yT[:, t, :], yT[:, t, :], rT[:, t, :], ALU.add))
                V.tensor_tensor(yT[:, t, :], yT[:, t, :], gT[:, t, :], ALU.mult).then_inc(sem("yg_ready"), 1)
            for m in range(KT):
                residual(base["WR"] + m, m)
            emptied(dve, base["WR"] + 7)
            dve.wait_ge(sem("shift_stored"), 16)
            dve.wait_ge(sem("p_wkv_out"), 16)
            norm(base["N4"], "nf1", "h_ready", 3)
            g = base["RL"]
            full(dve, g)
            lv3 = bank(g)[:, 0:24].rearrange("p (c e) -> p c e", c=3)
            V.tensor_copy(lg[:, 0:2, :], lv3[:, 0:2, :])
            V.tensor_copy(lg[0:TS, 2, :], lv3[0:TS, 2, :]).then_inc(freesem(g), 1)
            emptied(dve, g)
            io8 = C("iota")[:, 0:NE]
            for c, (t0, n) in enumerate(TOK):
                link(V.max(mx[0:n, c, :], lg[0:n, c, :]))
                link(V.max_index(ixu[0:n, c, :], mx[0:n, c, :], lg[0:n, c, :]))
                V.tensor_tensor(gt[0:n, c, 0:1], mx[0:n, c, 1:2], mx[0:n, c, 0:1], ALU.subtract)
                link(V.tensor_copy(ixf[0:n, c, :], ixu[0:n, c, :]))
                V.tensor_scalar(oh1[0:n, c, :], io8[0:n], ixf[0:n, c, 0:1], None, ALU.is_equal)
                link(V.tensor_scalar(oh2[0:n, c, :], io8[0:n], ixf[0:n, c, 1:2], None, ALU.is_equal))
                ins = V.tensor_tensor(selm[0:n, c, :], oh1[0:n, c, :], oh2[0:n, c, :], ALU.add)
            ins.then_inc(sem("gate_arg"), 1)
            dve.wait_ge(sem("gate_exp"), 1)
            for c, (t0, n) in enumerate(TOK):
                link(V.tensor_scalar(gt[0:n, c, 2:3], gt[0:n, c, 1:2], 1.0, None, ALU.add))
                link(V.reciprocal(gt[0:n, c, 2:3], gt[0:n, c, 2:3]))
                link(V.tensor_tensor(gt[0:n, c, 3:4], gt[0:n, c, 1:2], gt[0:n, c, 2:3], ALU.mult))
                link(V.tensor_scalar(comb[0:n, c, :], oh1[0:n, c, :], gt[0:n, c, 2:3], None, ALU.mult))
                link(V.scalar_tensor_tensor(comb[0:n, c, :], oh2[0:n, c, :], gt[0:n, c, 3:4], comb[0:n, c, :], ALU.mult, ALU.add))
            g = base["RK"]
            full(dve, g)
            rv = bank(g)[:, 0:24].rearrange("p (c e) -> p c e", c=3)
            for c, (t0, n) in enumerate(TOK):
                link(V.scalar_tensor_tensor(rank[0:n, c, :], rv[0:n, c, :], 1000.0, selm[0:n, c, :], ALU.add, ALU.mult))
                link(V.tensor_scalar(rank[0:n, c, :], rank[0:n, c, :], -1000.0, None, ALU.add))
                V.tensor_copy(rankJ[0:n, c, 0:NE], rank[0:n, c, :])
                V.tensor_copy(combJ[0:n, c, 0:NE], comb[0:n, c, :])
            V.tensor_copy(cntm, bank(g)[:, 24:32]).then_inc(freesem(g), 1)
            emptied(dve, g)
            V.tensor_scalar(flags[:, 0:8], cntm, 128.0, None, ALU.is_gt)
            V.tensor_copy(erow[:, 0:8], io8)
            V.tensor_copy(erow[:, 8:16], io8)
            link(V.tensor_scalar(flags[:, 8:16], cntm, 256.0, None, ALU.is_gt))
            link(V.tensor_tensor_scan(posn, C("ones")[:, 0:16], flags, 0.0, ALU.mult, ALU.add))
            V.tensor_scalar(jobf[:, 4:5], posn[:, 15:16], float(NE), None, ALU.add)
            for xj in range(4):
                link(V.tensor_scalar(ohx, posn, float(xj + 1), None, ALU.is_equal))
                link(V.tensor_tensor(ohx, ohx, flags, ALU.mult))
                link(V.tensor_tensor(tmpx, ohx, erow, ALU.mult))
                link(V.reduce_sum(jobf[:, xj:xj + 1], tmpx, AX))
                for c, (t0, n) in enumerate(TOK):
                    o2 = ohx[0:n].rearrange("p (a e) -> p a e", a=2)
                    t2 = tmpx[0:n].rearrange("p (a e) -> p a e", a=2)
                    link(V.tensor_tensor(t2, o2, comb[0:n, c, :].unsqueeze(1).broadcast_to([n, 2, NE]), ALU.mult))
                    link(V.reduce_sum(combJ[0:n, c, NE + xj:NE + xj + 1], tmpx[0:n], AX))
                    for p_ in range(2):
                        link(V.scalar_tensor_tensor(tmpx[0:n, 8 * p_:8 * p_ + 8], rank[0:n, c, :], -128.0 * (p_ + 1),
                                                    ohx[0:n, 8 * p_:8 * p_ + 8], ALU.add, ALU.mult))
                    link(V.reduce_sum(rankJ[0:n, c, NE + xj:NE + xj + 1], tmpx[0:n], AX))
            for t in (rankJ, combJ):
                V.memset(t[:, :, NJ:NJ + 1], -1000.0)
            V.tensor_copy(jobi[:, 0:5], jobf[:, 0:5]).then_inc(sem("jobs_ready"), 1)
            dve.wait_ge(sem("jobs_ready"), 1)
            dve.sem_inc(sem("gu_free"), 2)
            dve.sem_inc(sem("scattered"), 1)
            njobs = dve.value_load(jobi[0:1, 4:5], min_val=NE, max_val=NJ)

            def select(j):
                V.tensor_copy(cur[:, 0, 0:2], rankJ[:, 0:2, bass.ds(j, 1)].rearrange("p c a -> p (c a)"))
                V.tensor_copy(cur[0:TS, 0, 2:3], rankJ[0:TS, 2, bass.ds(j, 1)])
                V.tensor_copy(cur[:, 1, 0:2], combJ[:, 0:2, bass.ds(j, 1)].rearrange("p c a -> p (c a)"))
                V.tensor_copy(cur[0:TS, 1, 2:3], combJ[0:TS, 2, bass.ds(j, 1)]).then_inc(sem("cur_ready"), 1)
                dve.wait_ge(sem("cur_ready"), j + 1)
                for c, (t0, n) in enumerate(TOK):
                    V.tensor_scalar(Sel[0:n, c, :], C("iota")[0:n], cur[0:n, 0, c:c + 1], None, ALU.is_equal)
                    ins = V.tensor_scalar(Wsel[0:n, c, :], C("iota")[0:n], cur[0:n, 0, c:c + 1], cur[0:n, 1, c:c + 1],
                                          ALU.is_equal, ALU.mult)
                ins.then_inc(sem("sel_ready"), 1)

            def rests(j, c, part, pieces):
                s, n = c % MS, 2 if part == "gu" else 1
                for i in pieces:
                    o = i * 2048 + (GU if part == "dn" else 0)
                    dve.wait_ge(sem(f"{part}_head"), n * FC * j + n * c + i + 1)
                    V.tensor_tensor(mrest[s][:, o:o + 2048], mslot[s][:, o:o + 2048], mhead[c % 2][:, o:o + 2048].bitcast(F32),
                                    ALU.subtract).then_inc(sem(f"{part}_split"), 1)

            select(0)
            with dve.Fori(0, njobs) as j:
                rests(j, 0, "gu", range(2))
                for u in range(2):
                    dve.wait_ge(sem("hsel_head"), 2 * j + 1 + u)
                    hv = slice(4 * u, 4 * u + 4)
                    V.tensor_tensor(hsel[1][:, hv, :], ps[:, 5 + u, :].rearrange("p (k c) -> p k c", k=4),
                                    hsel[0][:, hv, :].bitcast(F32), ALU.subtract).then_inc(sem("gather_out"), 1)
                rests(j, 1, "gu", range(2))
                for c in range(FC + 1):
                    if c < FC:
                        dve.wait_ge(sem("silu_ready"), FC * j + c + 1)
                        if c >= 2:
                            dve.wait_ge(sem("tr_full"), FC * j + c - 1)
                        V.tensor_tensor(actm[c % 2], sgm, ps[:, c % 2, 256:512], ALU.mult).then_inc(sem("gu_free"), 1)
                    if c:
                        rests(j, c - 1, "dn", range(1))
                    if c + 2 < FC:
                        rests(j, c + 2, "gu", range(0, 1))
                    if c:
                        dve.wait_ge(sem("tr_head"), FC * j + c)
                        hd = actTm[(c - 1) % 2]
                        V.tensor_tensor(hd[1], ps[:, 2, 0:256], hd[0].bitcast(F32), ALU.subtract).then_inc(sem("tr_free"), 1)
                    if c + 2 < FC:
                        rests(j, c + 2, "gu", range(1, 2))
                    if c == FC // 2:
                        dve.wait_ge(sem("wt_ready"), j + 1)
                        select(j + 1)
                for m in range(KT):
                    dve.wait_ge(sem("scatter_full"), KT * j + m + 1)
                    V.tensor_tensor(x[:, m, :], x[:, m, :], ps[:, 5 + m % 3, 0:T], ALU.add).then_inc(sem("scattered"), 1)
                dve.wait_ge(sem("scattered"), KT * j + KT + 1)
            dve.sem_inc(sem("y_final"), 1)

        @block.tensor
        def _(pe):
            def take(g):
                if g >= 8:
                    pe.wait_ge(freesem(g), g // 8)
                return bank(g)

            def mm(o, l, r, start=True, stop=True, skip=False):
                return nc.tensor.matmul(o, l, r, start=start, stop=stop, skip_group_check=skip)

            def done(ins, g):
                ins.then_inc(fullsem(g), 1)

            def colsum(g, name, src, sems_, n0, ntiles=KT, t0=0):
                b = take(g)
                for k in range(ntiles):
                    pe.wait_ge(sem(sems_), n0 + k + 1)
                    ins = mm(b[:, 0:T], C(name), src[:, t0 + k, :], k == 0, k == ntiles - 1)
                done(ins, g)

            def proj(g, w, o, width, src, n=T, rows=P, kt=KT):
                b = take(g)
                for k in range(kt):
                    ins = mm(b[0:rows, 0:n], w[:, k, o:o + width], src[:, k, 0:n], k == 0, k == kt - 1)
                done(ins, g)

            pe.wait_ge(sem("cst_loaded"), 32)
            colsum(base["N1"], "ones", sq0, "sq_ready", 0)
            pe.wait_ge(sem("h_ready"), 1)
            wv = [W(f"win{c}").rearrange("p (k n) -> p k n", k=KT) for c in range(6)]
            for t in range(20):
                c, o = divmod(t * 128, 768)
                if o == 0:
                    loaded(pe, f"win{c}")
                g = base["Z"] + t if t < 8 else base["X"] + t - 8
                proj(g, wv[c], o, P, h)
            proj(base["DT"], wv[3], 256, 16, h, rows=16)
            for t in range(8):
                c, o = divmod(t * 128, 768)
                if o == 0:
                    loaded(pe, f"win{4 + c}")
                proj(base["Q"] + t, wv[4 + c], o, P, h)
            for j in range(NKV):
                g = base["K"] + j
                b = take(g)
                for k in range(KT):
                    kw = wv[5][:, k, 256 + j * HD:256 + (j + 1) * HD]
                    for par in range(2):
                        ins = mm(b[64 * par:64 * par + 64, 0:T], kw, h[:, k, :], k == 0, k == KT - 1)
                done(ins, g)
            for c, (t0, n) in enumerate(TOK):
                g = base["V"] + c
                b = take(g)
                for k in range(KT):
                    ins = mm(b[0:n, 0:256], h[:, k, t0:t0 + n], wv[5][:, k, 512:768], k == 0, k == KT - 1)
                done(ins, g)
            for t in range(12):
                g = base["QN"] + t
                emptied(pe, base["Q"] + t)
                b = take(g)
                done(mm(b[:, 0:T], C("blk64"), qksq[:, t, :]), g)
            pe.wait_ge(sem("sc_ready"), 1)
            g = base["TT"]
            b = take(g)
            for c, (t0, n) in enumerate(TOK):
                ins = nc.tensor.transpose(b[0:n, c * 96:(c + 1) * 96], SC[0:96, t0:t0 + n], C("ident")[0:96, 0:96])
            done(ins, g)
            pe.wait_ge(sem("xc_ready"), CT)
            emptied(pe, base["QN"] + 11)
            for c, (t0, n) in enumerate(TOK):
                for hf in range(2):
                    g = base["XT"] + 2 * c + hf
                    b = take(g)
                    for i in range(4):
                        ins = nc.tensor.transpose(b[0:n, i * P:(i + 1) * P], xc[:, 4 * hf + i, t0:t0 + n], ident)
                    done(ins, g)
            for u in range(2):
                g = base["BT"] + u
                b = take(g)
                for c in ((0, 1) if u == 0 else (2,)):
                    t0, n = TOK[c]
                    for gg in range(2):
                        o = (c % 2) * 256 + gg * P
                        ins = nc.tensor.transpose(b[0:n, o:o + P], xc[:, 8 + gg, t0:t0 + n], ident)
                done(ins, g)
            g = base["CB"]
            b = take(g)
            for c in range(2):
                for gg in range(2):
                    ins = mm(b[:, (2 * c + gg) * P:(2 * c + gg + 1) * P], xc[:, 8 + gg, c * P:(c + 1) * P],
                             xc[:, 10 + gg, c * P:(c + 1) * P])
            done(ins, g)
            g += 1
            b = take(g)
            for gg in range(2):
                ins = mm(b[0:TS, gg * TS:(gg + 1) * TS], xc[:, 8 + gg, TP:T], xc[:, 10 + gg, TP:T])
            done(ins, g)
            emptied(pe, base["BT"])
            for gg in range(2):
                g = base["H1"] + gg
                emptied(pe, base["XT"] + gg)
                b = take(g)
                done(mm(b[:, :], Btok[:, 0, gg * P:(gg + 1) * P], xdec[:, 0, gg * 512:(gg + 1) * 512]), g)

            def spread(out_, hh, t0, n):
                return mm(out_, C("ident")[0:16, hh:hh + 1].broadcast_to([16, P]), acs[0:16, t0:t0 + n])

            g = base["ES"]
            b = take(g)
            for hh in range(NH):
                ins = spread(b[:, hh * TS:(hh + 1) * TS], hh, TP, TS)
            done(ins, g)
            pe.wait_ge(sem("es_done"), 1)
            emptied(pe, base["H1"])
            emptied(pe, base["H1"] + 1)
            emptied(pe, base["XT"] + 5)
            loaded(pe, "ssm0")
            for qd in range(4):
                for c in range(2):
                    g = base[f"E{qd}"] + c
                    b = take(g)
                    for k in range(4):
                        ins = spread(b[:, k * P:(k + 1) * P], 4 * qd + k, c * P, P)
                    done(ins, g)
                if qd == 2:
                    loaded(pe, "ssm1")
                pe.wait_ge(sem("cs_ready"), qd + 1)
                for u in range(2):
                    i = 2 * qd + u
                    g = base[f"Y{qd}"] + u
                    b = take(g)
                    for par in range(2):
                        hh = 2 * i + par
                        r0 = 64 * par
                        kk_ = hh % 4
                        ho = slice(hh * HD, (hh + 1) * HD)
                        e0, e1 = Eb[(2 * qd) % 4], Eb[(2 * qd + 1) % 4]
                        kq = slice(kk_ * P, (kk_ + 1) * P)
                        mm(b[r0:r0 + 64, 0:P], xdt[:, 0, ho], e0[:, kq])
                        mm(b[r0:r0 + 64, P:2 * P], xdt[:, 1, ho], e1[:, kq], True, False)
                        mm(b[r0:r0 + 64, P:2 * P], H1T[:, ho], expq[qd % 2][:, kq], False, True)
                        mm(b[r0:r0 + 64, TP:T], xdt[0:TS, 2, ho], Ms[:, hh, :], True, True, skip=True)
                        sv = W(f"ssm{hh // 8}").rearrange("p (b n) -> p b n", b=DB)
                        for s in range(DB):
                            ins = mm(b[r0:r0 + 64, TP + DL * s:TP + DL * (s + 1)], sv[:, s, (hh % 8) * HD:(hh % 8 + 1) * HD],
                                     CsS[:, hh, DL * s:DL * (s + 1)], False, True, skip=True)
                    done(ins, g)
            for gg in range(2):
                g = base["FP"] + gg
                b = take(g)
                done(mm(b[:, :], Btok[:, 1, gg * P:(gg + 1) * P], xdec[:, 1, gg * 512:(gg + 1) * 512]), g)
            pe.wait_ge(sem("Bm_ready"), 1)
            for gg in range(2):
                for s in range(DB):
                    g = base["FS"] + gg * DB + s
                    b = take(g)
                    done(mm(b[:, :], Bm[0:TS, s, gg * P:(gg + 1) * P], xdec[0:TS, 2, gg * 512:(gg + 1) * 512]), g)
            for gg in range(2):
                colsum(base["YN"] + gg, "ones", ysq, "sq_ready", 8 + 4 * gg, 4, 4 * gg)
            pe.wait_ge(sem("q_normed"), 8)
            pe.wait_ge(sem("k_normed"), 4)
            for j in range(5):
                if j < 4:
                    for u in range(4):
                        g = base[f"S{j}"] + u
                        b = take(g)
                        r0 = 64 * (u % 2)
                        q0, nk = 128 * (u // 2), 128 * (u // 2 + 1)
                        for n in range(2):
                            ins = mm(b[:, n * nk:(n + 1) * nk], qT[r0:r0 + 64, 2 * j + n, q0:q0 + 128], kT[r0:r0 + 64, j, 0:nk])
                        done(ins, g)
                if j > 0:
                    jj = j - 1
                    s = jj % 2
                    pe.wait_ge(sem("p_ready"), jj + 1)
                    for u in range(3):
                        g = base[f"PT{jj}"] + u
                        b = take(g)
                        for n in range(4):
                            o = u * 512 + n * 128
                            ins = nc.tensor.transpose(b[:, n * P:(n + 1) * P], PP[s][:, o:o + 128], ident)
                        done(ins, g)
                    for u in range(3):
                        emptied(pe, base[f"PT{jj}"] + u)
                    for u in range(2):
                        g = base[f"O{jj}"] + u
                        b = take(g)
                        for par in range(2):
                            r0 = 64 * par
                            n = 2 * u + par
                            vv = [vtok[:, c, jj * HD:(jj + 1) * HD] for c in range(2)]
                            mm(b[r0:r0 + 64, 0:P], vv[0], PT[s][:, n * P:(n + 1) * P])
                            for c in range(2):
                                o = 512 + n * 256 + c * P
                                ins = mm(b[r0:r0 + 64, P:2 * P], vv[c], PT[s][:, o:o + P], c == 0, c == 1)
                        done(ins, g)
            loaded(pe, "kv")
            kvs = W("kv")
            kc = kvs[:, 0:4096].rearrange("p (b j k) -> p b j k", b=DB, j=NKV)
            vc = kvs[:, 4096:6144].rearrange("p (b n) -> p b n", b=DB)
            for par in range(2):
                r0 = 64 * par
                g = base["SS"] + par
                b = take(g)
                b4 = b[:, 0:256].rearrange("p (b i l) -> p b i l", b=DB, i=8)
                for s in range(DB):
                    for j in range(NKV):
                        ins = mm(b4[:, s, 2 * j:2 * j + 2, :], kc[r0:r0 + 64, s, j, :],
                                 qT[r0:r0 + 64, 2 * j:2 * j + 2, TP + DL * s:TP + DL * (s + 1)])
                done(ins, g)
            for par in range(2):
                r0 = 64 * par
                g = base["SS"] + 2 + par
                b = take(g)
                b4 = b[:, 0:256].rearrange("p (b i l) -> p b i l", b=DB, i=8)
                for i in range(8):
                    ins = mm(b4[0:TS, :, i, :], kT[r0:r0 + 64, i // 2, TP:T],
                             qT[r0:r0 + 64, i, TP:T].rearrange("p (b l) -> p b l", l=DL))
                done(ins, g)
            for u in range(4):
                emptied(pe, base["SS"] + u)
            for u in range(2):
                g = base["ST"] + u
                b = take(g)
                for w in range(2):
                    jj = 2 * u + w
                    nc.tensor.transpose(b[:, w * 160:w * 160 + 128], SA[:, jj * P:(jj + 1) * P], ident)
                    ins = nc.tensor.transpose(b[:, w * 160 + 128:w * 160 + 160], SBn[:, jj * P:(jj + 1) * P], C("ident")[0:TS, 0:TS])
                done(ins, g)
            pe.wait_ge(sem("ps_ready"), 1)
            g = base["PTS"]
            b = take(g)
            for jj in range(4):
                ins = nc.tensor.transpose(b[:, jj * P:(jj + 1) * P], PS[:, jj, 0:128], ident)
            done(ins, g)
            g += 1
            b = take(g)
            for jj in range(4):
                ins = nc.tensor.transpose(b[0:TS, jj * P:(jj + 1) * P], PS[:, jj, 128:160], ident)
            done(ins, g)
            emptied(pe, base["PTS"])
            emptied(pe, base["PTS"] + 1)
            g = base["OS"]
            b = take(g)
            ob = b[:, 0:256].rearrange("p (i b l) -> p i b l", i=8, b=DB)
            pa4 = PTA.rearrange("p (b i r l) -> p b i r l", b=DB, i=8, r=2)
            for s in range(DB):
                for j in range(NKV):
                    for par in range(2):
                        r0 = 64 * par
                        ins = mm(ob[r0:r0 + 64, 2 * j:2 * j + 2, s, :], vc[:, s, j * HD:(j + 1) * HD],
                                 pa4[:, s, 2 * j:2 * j + 2, par, :])
            done(ins, g)
            g += 1
            b = take(g)
            pb4 = PTB.rearrange("p (b h l) -> p b h l", b=DB, h=NH)
            for hh in range(NH):
                r0 = 64 * (hh % 2)
                i = hh // 2
                ins = mm(b[r0:r0 + 64, i * TS:(i + 1) * TS].rearrange("p (b l) -> p b l", l=DL),
                         vtok[0:TS, 2, (hh // 4) * HD:(hh // 4 + 1) * HD], pb4[:, :, hh, :])
            done(ins, g)
            pe.wait_ge(sem("yssd_ready"), 1)
            emptied(pe, base["OS"] + 1)
            for m in range(KT):
                c, o = divmod(m * P, 384)
                if o == 0:
                    loaded(pe, f"wout{c}")
                w = W(f"wout{c}").rearrange("p (k n) -> p k n", k=16)
                g = base["WO"] + m
                b = take(g)
                for k in range(16):
                    src = z[:, k, :] if k < 8 else oT[:, k - 8, :]
                    ins = mm(b[:, 0:T], w[:, k, o:o + P], src, k == 0, k == 15)
                done(ins, g)
            colsum(base["N2"], "ones", sq2, "sq_ready", 16)
            for c in range(FC + 1):
                if c < FC:
                    pe.wait_ge(sem("ffn_gu_split"), 2 * c + 2)
                    o0, h0 = (where[f"ffn{c}"] % RING) * SLOT, (c % 2) * SLOT
                    wh, wr = (t.rearrange("p (k s n) -> p s k n", s=2, k=KT) for t in
                              (mhead_[:, h0:h0 + GU], rest_ring[:, o0:o0 + GU]))
                    for u in range(2):
                        us = slice(u * P, (u + 1) * P)
                        for s in range(2):
                            g = base[f"FU{c}"] + 2 * u + s
                            b = take(g)
                            for k in range(KT):
                                if c + u + s == 0:
                                    pe.wait_ge(sem("h_split"), k + 1)
                                mm(b[:, 0:T], wh[:, s, k, us], hsplit[0][:, k, :], k == 0, False)
                                mm(b[:, 0:T], wh[:, s, k, us], hsplit[1][:, k, :], False, False)
                                ins = mm(b[:, 0:T], wr[:, s, k, us], hsplit[0][:, k, :], False, k == KT - 1)
                            done(ins, g)
                if c:
                    cd = c - 1
                    pe.wait_ge(sem("ffn_dn_split"), cd + 1)
                    pe.wait_ge(sem("act_split"), 2 * cd + 2)
                    o0, h0 = (where[f"ffn{cd}"] % RING) * SLOT + GU, (cd % 2) * SLOT + GU
                    wh, wr = (t.rearrange("p (u n) -> p u n", u=2) for t in
                              (mhead_[:, h0:h0 + SLOT - GU], rest_ring[:, o0:o0 + SLOT - GU]))
                    for m in range(KT):
                        g = base[f"FD{cd}"] + m
                        ms = slice(m * P, (m + 1) * P)
                        b = take(g)
                        for u in range(2):
                            ah, an = actT[(2 * cd + u) % 4]
                            mm(b[:, 0:T], wh[:, u, ms], ah, u == 0, False)
                            mm(b[:, 0:T], wh[:, u, ms], an, False, False)
                            ins = mm(b[:, 0:T], wr[:, u, ms], ah, False, u == 1)
                        done(ins, g)
            colsum(base["N3"], "ones", sq3, "sq_ready", 24)
            for n, nm in enumerate("rkv"):
                pe.wait_ge(sem("xi_ready"), 8 * n + 8)
                for hf in range(2):
                    loaded(pe, f"w{nm}{hf}")
                    w = W(f"w{nm}{hf}").rearrange("p (k n) -> p k n", k=KT)
                    for m in range(4):
                        proj(base["R" + nm] + 4 * hf + m, w, m * P, P, xi[n % 2])
            loaded(pe, "lora")
            lw = W("lora")
            l1 = {"w": (0, 64), "a": (512, 64), "g": (1024, 128)}
            l2 = {"w": 2048, "a": 3072, "g": 4096}
            for n, nm in enumerate("wag"):
                pe.wait_ge(sem("xi_ready"), 8 * (n + 3) + 8)
                o, rows = l1[nm]
                w = lw[:, o:o + KT * rows].rearrange("p (k n) -> p k n", k=KT)
                proj(base["H" + nm], w, 0, rows, xi[(n + 3) % 2], rows=rows)
                emptied(pe, base["H" + nm])
                for m in range(KT):
                    g = base["R" + nm] + m
                    b = take(g)
                    done(mm(b[:, 0:T], lw[0:rows, l2[nm] + m * P:l2[nm] + (m + 1) * P], hid[n % 2][0:rows, :]), g)
            for t in range(KT):
                g = base["KN"] + t
                pe.wait_ge(sem("kksq_ready"), t + 1)
                b = take(g)
                done(mm(b[:, 0:T], C("blk64"), tm1[t % 2]), g)
            for t in range(KT):
                g = base["BO"] + t
                pe.wait_ge(sem("bonus_ready"), t + 1)
                b = take(g)
                done(mm(b[:, 0:T], C("blk64"), tm1[t % 2]), g)
            pe.wait_ge(sem("tilde_ready"), KT)
            emptied(pe, base["BO"] + 7)
            pe.wait_ge(sem("st_ready"), 1)

            def token_major(name, c):
                t0, n = TOK[c]
                for u, src in enumerate((vT, aT, k1)):
                    for hf in range(2):
                        g = base[name] + 2 * u + hf
                        b = take(g)
                        for i in range(4):
                            ins = nc.tensor.transpose(b[0:n, i * P:(i + 1) * P], src[:, 4 * hf + i, t0:t0 + n], ident)
                        done(ins, g)

            for c in range(2):
                t0 = c * P
                token_major(f"VT{c}", c)
                for hh in range(2):
                    idx = 2 * c + hh
                    for n in range(8):
                        hd = 8 * hh + n
                        i, r0 = hd // 2, 64 * (hd % 2)
                        g = base[f"A{c}{hh}"] + n
                        b = take(g)
                        for u, src in enumerate((aT, k1)):
                            ins = mm(b[:, 256 * u:256 * u + 256].rearrange("p (a t) -> p a t", a=2),
                                     src[r0:r0 + 64, i, t0:t0 + P], AR[r0:r0 + 64, i, :, t0:t0 + P])
                        done(ins, g)
                    for q in range(2):
                        g = base[f"X{c}{hh}"] + q
                        b = take(g)
                        for n in range(4):
                            i, r0 = 4 * hh + n, 64 * q
                            ins = mm(b[:, n * P:(n + 1) * P], AR[r0:r0 + 64, i, 0, t0:t0 + P], aT[r0:r0 + 64, i, t0:t0 + P])
                        done(ins, g)
                    pe.wait_ge(sem("m0_ready"), 2 * idx + 2)
                    for lv in range(1, 6):
                        lys, lms, lts = (base.get(f"{nm}{c}{hh}{lv}") for nm in ("LY", "LM", "LT"))
                        for q in range(2):
                            pe.wait_ge(sem("xl_ready"), 10 * idx + 2 * (lv - 1) + q + 1)
                            if lv > 1:
                                emptied(pe, base[f"LM{c}{hh}{lv - 1}"] + q)
                                emptied(pe, base[f"LT{c}{hh}{lv - 1}"] + q)
                            b = take(lys + q)
                            for n in range(4):
                                ins = mm(b[:, n * P:(n + 1) * P], Xl[:, 4 * q + n, :], Mi[:, 4 * q + n, :])
                            done(ins, lys + q)
                        for q in range(2):
                            emptied(pe, lys + q)
                            b = take(lms + q)
                            for n in range(4):
                                ins = mm(b[:, n * P:(n + 1) * P], Mti[:, 4 * q + n, :], Yi[:, 4 * q + n, :])
                            done(ins, lms + q)
                        if lts is not None:
                            for q in range(2):
                                b = take(lts + q)
                                for n in range(4):
                                    ins = mm(b[:, n * P:(n + 1) * P], Yi[:, 4 * q + n, :], Mti[:, 4 * q + n, :])
                                done(ins, lts + q)
                    emptied(pe, base[f"LM{c}{hh}5"])
                    emptied(pe, base[f"LM{c}{hh}5"] + 1)
                    for u in range(6):
                        emptied(pe, base[f"VT{c}"] + u)
                    for cc in range(2):
                        g = base[f"q{c}{hh}{cc}"]
                        tb = 64 * cc
                        tk = t0 + tb
                        tr = slice(tb, tb + 64)
                        if cc or c:
                            pe.wait_ge(sem("st_ready"), (4 * c + 2 * hh + cc) + 1 if cc else 4 + 1)
                        heads = [(n, (8 * hh + n) // 2, 64 * (n % 2), (8 * hh + n) * HD) for n in range(8)]
                        b = take(g)
                        pairs = range(4 * hh, 4 * hh + 4)
                        for i in pairs:
                            mm(b[tr, (i % 4) * P:(i % 4 + 1) * P], AR[:, i, 0, tk:tk + 64],
                               Sd[:, i].rearrange("p r v -> p (r v)"), i % 4 == 0, True, skip=True)
                        for n, i, r0, ho in heads:
                            ins = mm(b[tr, n * HD:(n + 1) * HD], A4[tr, n, 2, tr], v1[tr, ho:ho + HD], False, True, skip=True)
                        done(ins, g)
                        emptied(pe, g)
                        b = take(g + 1)
                        for n, i, r0, ho in heads:
                            ins = mm(b[tr, n * HD:(n + 1) * HD], Mi[tr, n, tr], Zs[tr, n * HD:(n + 1) * HD])
                        done(ins, g + 1)
                        emptied(pe, g + 1)
                        b = take(g + 2)
                        for i in pairs:
                            mm(b[:, (i % 4) * 64:(i % 4 + 1) * 64], Sd[:, i].rearrange("p r v -> p (r v)"),
                               AR[:, i, 1, tk:tk + 64], i % 4 == 0, True, skip=True)
                        for n, i, r0, ho in heads:
                            o = b[r0:r0 + 64, (i % 4) * 64:(i % 4 + 1) * 64]
                            mm(o, Us[tr, n * HD:(n + 1) * HD], A4[tr, n, 1, tr], False, True, skip=True)
                            ins = mm(o, v1[tr, ho:ho + HD], A4[tr, n, 3, tr], False, True, skip=True)
                        done(ins, g + 2)
                        b = take(g + 3)
                        for n, i, r0, ho in heads:
                            o = b[r0:r0 + 64, (i % 4) * 64:(i % 4 + 1) * 64]
                            mm(o, b1[tr, ho:ho + HD], Us[tr, n * HD:(n + 1) * HD], True, False)
                            ins = mm(o, k1t[tr, ho:ho + HD], v1[tr, ho:ho + HD], False, True)
                        done(ins, g + 3)
            token_major("sVT", 2)
            for q in range(4):
                g = base["sA"] + q
                b = take(g)
                for n in range(4):
                    i, r0 = 4 * (q // 2) + n, 64 * (q % 2)
                    for u, src in enumerate((aT, k1)):
                        ins = mm(b[0:TS, n * P + 64 * u:n * P + 64 * u + 64].rearrange("p (a t) -> p a t", a=2),
                                 src[r0:r0 + 64, i, TP:T], AR[r0:r0 + 64, i, :, TP:T])
                done(ins, g)
            for par in range(2):
                g = base["sX"] + par
                b = take(g)
                for i in range(8):
                    r0 = 64 * par
                    ins = mm(b[0:TS, i * TS:(i + 1) * TS], AR[r0:r0 + 64, i, 0, TP:T], aT[r0:r0 + 64, i, TP:T])
                done(ins, g)
            pe.wait_ge(sem("m2_ready"), 1)
            g = base["sL"]
            b = take(g)
            for hd in range(NH):
                ins = mm(b[0:TS, hd * TS:(hd + 1) * TS], Xl2[:, hd, :], M2[:, hd, :])
            done(ins, g)
            emptied(pe, g)
            b = take(g + 1)
            for hd in range(NH):
                ins = mm(b[0:TS, hd * TS:(hd + 1) * TS], Mt2[:, hd, :], Yi2[:, hd, :])
            done(ins, g + 1)
            loaded(pe, "wkv")
            wk = W("wkv").rearrange("p (k b v) -> p k b v", k=KT, b=DB)
            g = base["sZY"]
            b = take(g)
            zy = b.rearrange("p (n a l) -> p n a l", a=2, l=DL)
            for i in range(KT):
                for r0 in (0, 64):
                    for s in range(DB):
                        ins = mm(zy[r0:r0 + 64, i * DB + s], wk[r0:r0 + 64, i, s, :],
                                 AR[r0:r0 + 64, i, :, TP + DL * s:TP + DL * (s + 1)])
            done(ins, g)
            emptied(pe, g)
            emptied(pe, base["sL"] + 1)
            for u in range(6):
                emptied(pe, base["sVT"] + u)
            for hh in range(2):
                g = base["sZ"] + hh
                b = take(g)
                for i in range(4 * hh, 4 * hh + 4):
                    mm(b[0:TS, (i % 4) * P:(i % 4 + 1) * P], z1T[:, i, :], ident, True, True, skip=True)
                    for par in range(2):
                        hd = 2 * i + par
                        o = (i % 4) * P + par * HD
                        ins = mm(b[0:TS, o:o + HD], A4s[:, hd, 2, :], v1[0:TS, hd * HD:(hd + 1) * HD], False, True, skip=True)
                done(ins, g)
            for hh in range(2):
                emptied(pe, base["sZ"] + hh)
                g = base["sU"] + hh
                b = take(g)
                for n in range(8):
                    hd = 8 * hh + n
                    ins = mm(b[0:TS, n * HD:(n + 1) * HD], M2[:, hd, :], Zs2[:, hd * HD:(hd + 1) * HD])
                done(ins, g)
            for hd in range(NH):
                g = base["sS"] + hd
                r0 = 64 * (hd % 2)
                pe.wait_ge(sem("uvm_ready"), hd + 1)
                b = take(g)
                done(mm(b[r0:r0 + 64, :].rearrange("p (b v) -> p b v", b=DB), BK[:, hd * HD:(hd + 1) * HD], UVm[hd % 2]), g)
            g = base["sY"]
            b = take(g)
            for hd in range(NH):
                i, r0 = hd // 2, 64 * (hd % 2)
                o = b[r0:r0 + 64, i * TS:(i + 1) * TS]
                mm(o, UV[0:TS, hd * HD:(hd + 1) * HD], A4s[:, hd, 1, :], True, False)
                ins = mm(o, v1[0:TS, hd * HD:(hd + 1) * HD], A4s[:, hd, 3, :], False, True)
            done(ins, g)
            emptied(pe, g)
            emptied(pe, base["q111"] + 2)
            for nm, sname, src in (("GM", None, None), ("GV", "ysq_ready", tm1)):
                for t in range(KT):
                    g = base[nm] + t
                    if sname:
                        pe.wait_ge(sem(sname), t + 1)
                    b = take(g)
                    done(mm(b[:, 0:T], C("blk64"), tm1[t % 2] if sname else yT[:, t, :]), g)
            pe.wait_ge(sem("yg_ready"), KT)
            for hf in range(2):
                loaded(pe, f"wo{hf}")
                w = W(f"wo{hf}").rearrange("p (k n) -> p k n", k=KT)
                for m in range(4):
                    proj(base["WR"] + 4 * hf + m, w, m * P, P, yT)
            colsum(base["N4"], "ones", xi[0], "sq_ready", 32)
            pe.wait_ge(sem("h_ready"), 3)
            for c, (t0, n) in enumerate(TOK):
                for hf in range(2):
                    g = base["HT"] + 2 * c + hf
                    b = take(g)
                    for i in range(4):
                        ins = nc.tensor.transpose(b[0:n, i * P:(i + 1) * P], h[:, 4 * hf + i, t0:t0 + n], ident)
                    done(ins, g)
            pe.wait_ge(sem("router_loaded"), 16)
            r3 = rt[:, :].rearrange("p (k e) -> p k e", k=KT)
            g = base["RL"]
            b = take(g)
            for c, (t0, n) in enumerate(TOK):
                for k in range(KT):
                    ins = mm(b[0:n, c * NE:(c + 1) * NE], h[:, k, t0:t0 + n], r3[:, k, :], k == 0, k == KT - 1)
            done(ins, g)
            pe.wait_ge(sem("gate_arg"), 1)
            g = base["RK"]
            b = take(g)
            for c, (t0, n) in enumerate(TOK):
                for c2 in range(c + 1):
                    l = C("strict")[0:n, 0:n] if c2 == c else C("ones")[:, 0:n]
                    mm(b[0:n, c * NE:(c + 1) * NE], l, selm[0:TOK[c2][1], c2, :], c2 == 0, c2 == c)
            for c, (t0, n) in enumerate(TOK):
                ins = mm(b[:, 24:32], C("ones")[0:n, :], selm[0:n, c, :], c == 0, c == 2)
            done(ins, g)
            emptied(pe, base["RK"])
            for u in range(6):
                emptied(pe, base["HT"] + u)
            pe.wait_ge(sem("jobs_ready"), 1)
            njobs = pe.value_load(jobi[0:1, 4:5], min_val=NE, max_val=NJ)
            with pe.Fori(0, njobs) as j:
                pe.wait_ge(sem("sel_ready"), j + 1)
                pe.wait_ge(sem("scattered"), KT * j + 1)
                for u in range(2):
                    for k in range(4):
                        for c, (t0, n) in enumerate(TOK):
                            kk = 4 * u + k
                            ins = mm(ps[:, 5 + u, k * P:(k + 1) * P], htok[0:n, c, kk * P:(kk + 1) * P], Sel[0:n, c, :],
                                     c == 0, c == 2)
                    ins.then_inc(sem("gather_full"), 1)
                for c, (t0, n) in enumerate(TOK):
                    ins = nc.tensor.transpose(ps[:, 7, t0:t0 + n], Wsel[0:n, c, :], C("ident")[0:n, 0:n])
                ins.then_inc(sem("gather_full"), 1)

                def up(c):
                    s = c % MS
                    pe.wait_ge(sem("gu_split"), 2 * FC * j + 2 * c + 2)
                    pe.wait_ge(sem("gu_free"), FC * j + c + 1)
                    wh, wr = (t[:, 0:GU].rearrange("p (k n) -> p k n", k=KT) for t in (mhead[c % 2], mrest[s]))
                    hh, hr = hsel
                    for k in range(KT):
                        if c == 0 and k % 4 == 0:
                            pe.wait_ge(sem("gather_out"), 2 * j + k // 4 + 1)
                        mm(ps[:, c % 2, :], hh[:, k, :], wh[:, k, :], k == 0, False)
                        mm(ps[:, c % 2, :], hh[:, k, :], wr[:, k, :], False, False)
                        ins = mm(ps[:, c % 2, :], hr[:, k, :], wh[:, k, :], False, k == KT - 1)
                    ins.then_inc(sem("gu_full"), 1)

                def turn(c):
                    pe.wait_ge(sem("gu_free"), FC * j + c + 3)
                    if c >= 1:
                        pe.wait_ge(sem("tr_free"), FC * j + c)
                    for u in range(2):
                        ins = nc.tensor.transpose(ps[:, 2, u * P:(u + 1) * P], actm[c % 2][:, u * P:(u + 1) * P], ident)
                    ins.then_inc(sem("tr_full"), 1)

                def down(c):
                    s = c % MS
                    pe.wait_ge(sem("tr_free"), FC * j + c + 1)
                    pe.wait_ge(sem("dn_split"), FC * j + c + 1)
                    wh, wr = (t[:, GU:SLOT].rearrange("p (u n) -> p u n", u=2) for t in (mhead[c % 2], mrest[s]))
                    ah, an = actTm[c % 2]
                    for u in range(2):
                        us = slice(u * P, (u + 1) * P)
                        first, last = c == 0 and u == 0, c == FC - 1 and u == 1
                        for hf in range(2):
                            cols_ = slice(hf * 512, (hf + 1) * 512)
                            mm(ps[:, 3 + hf, :], ah[:, us], wh[:, u, cols_], first, False)
                            mm(ps[:, 3 + hf, :], ah[:, us], wr[:, u, cols_], False, False)
                            ins = mm(ps[:, 3 + hf, :], an[:, us], wh[:, u, cols_], False, last)
                    ins.then_inc(sem(f"dn_slot_free{s}"), 1)

                for c in range(FC + 2):
                    if c < FC:
                        up(c)
                    if c >= 2:
                        down(c - 2)
                    if 1 <= c <= FC:
                        turn(c - 1)
                for m in range(KT):
                    if m == 0:
                        pe.wait_ge(sem("y_out"), j + 1)
                        pe.wait_ge(sem("wt_ready"), j + 1)
                    if m >= 3:
                        pe.wait_ge(sem("scattered"), KT * j + m - 1)
                    mm(ps[:, 5 + m % 3, 0:T], ysb[:, m * P:(m + 1) * P], Wt).then_inc(sem("scatter_full"), 1)


def kernel(**inp):
    import concourse.bacc as bacc
    from concourse.bass_utils import run_bass_kernel_spmd as run

    f = {k: np.asarray(w) for k, w in inp.items()}

    def cols(w):
        return np.ascontiguousarray(w.reshape(-1, P).T)

    def kmajor(w):
        return w.reshape(-1, P, w.shape[-1]).transpose(1, 0, 2)

    def chunks(w, cuts):
        full = kmajor(w)
        widest = max(n for _, n in cuts)
        a = np.zeros((len(cuts), P, full.shape[1] * widest), np.float32)
        for i, (c0, n) in enumerate(cuts):
            a[i, :, :full.shape[1] * n] = full[:, :, c0:c0 + n].reshape(P, -1)
        return a

    def ff_chunks(g, u, d):
        g4 = g.reshape(KT, P, FC, 256).transpose(2, 1, 0, 3)
        u4 = u.reshape(KT, P, FC, 256).transpose(2, 1, 0, 3)
        gu = np.concatenate([g4, u4], 3).reshape(FC, P, 4096)
        dd = d.reshape(FC, 2, P, D).transpose(0, 2, 1, 3).reshape(FC, P, 2048)
        return np.concatenate([gu, dd], 2)

    xs = np.concatenate([f["x_prompt"].reshape(TP, D), f["x_sample"].reshape(TS, D)], 0)
    arrays = {"x_fm": kmajor(np.ascontiguousarray(xs.T)).reshape(P, KT * T)}
    parts = {"nm0": cols(f["norm_mix"][0]), "nm1": cols(f["norm_mix"][1]), "nf0": cols(f["norm_ffn"][0]),
             "nf1": cols(f["norm_ffn"][1]), "ssdn": cols(f["ssd_norm"][0]),
             "convw": f["conv_w"][0].reshape(4, CT, P).transpose(2, 1, 0).reshape(P, 48), "convb": cols(f["conv_b"][0]),
             "dskip": cols(np.repeat(f["d_skip"][0], HD)), "qn": np.tile(f["q_norm"][0], 2)[:, None],
             "kn": np.tile(f["k_norm"][0], 2)[:, None], "mu": cols(f["rwkv_mu"][0]), "w0": cols(f["rwkv_w0"][0]),
             "a0": cols(f["rwkv_a0"][0]), "kk": cols(f["rwkv_kk"][0]), "ka": cols(f["rwkv_ka"][0]),
             "rk": cols(f["rwkv_rk"][0]), "lnw": cols(f["rwkv_ln_w"][0]), "lnb": cols(f["rwkv_ln_b"][0]),
             "sinks": np.tile(f["attn_sinks"][0], (P, 1)),
             "sinkrow": np.tile(np.repeat(f["attn_sinks"][0], DL), 2)[:, None],
             "dtb": np.tile(f["dt_bias"][0], 8)[:, None], "alog": np.tile(f["a_log"][0], 8)[:, None]}
    arrays["vecs"] = np.concatenate([parts[n] for n in VEC], 1)
    arrays["consts"] = CONSTS
    arrays["attn_masks"] = ATTN_MASKS
    arrays["w_in"] = chunks(f["w_in"][0], W_IN_CHUNKS)
    arrays["w_out"] = chunks(f["w_out"][0], W_OUT_CHUNKS)
    arrays["ffn_w"] = ff_chunks(f["ffn_gate"][0], f["ffn_up"][0], f["ffn_down"][0])
    arrays["moe_w"] = np.stack([ff_chunks(f["moe_gate"][0, e], f["moe_up"][0, e], f["moe_down"][0, e]) for e in range(NE)])
    halves = [(0, 512), (512, 512)]
    for n in ("wr", "wk", "wv", "wo"):
        arrays[n] = chunks(f["rwkv_" + n][0], halves)
    lora = np.zeros((P, 5120), np.float32)
    for n, o, w in (("w1", 0, 64), ("a1", 512, 64), ("g1", 1024, 128)):
        lora[:, o:o + KT * w] = kmajor(f["rwkv_" + n][0]).reshape(P, -1)
    for n, o in (("w2", 2048), ("a2", 3072), ("g2", 4096)):
        w = f["rwkv_" + n][0]
        lora[:w.shape[0], o:o + D] = w
    arrays["lora"] = lora
    arrays["router"] = kmajor(f["moe_router"][0]).reshape(P, -1)
    arrays["convT"] = f["state_conv"][0].reshape(24, CT, P).transpose(2, 1, 0).reshape(P, CT * 24)
    arrays["ssmT"] = f["state_ssm"][0].reshape(DB, 2, 8, HD, P).transpose(1, 4, 0, 2, 3).reshape(2, P, 4096)
    kc, vc = f["cache_swa_k"][0], f["cache_swa_v"][0]
    kt_ = kc.transpose(3, 0, 2, 1).reshape(HD, DB * NKV * P)
    arrays["kv_cache"] = np.concatenate([np.concatenate([kt_, kt_], 0), vc.transpose(1, 0, 2, 3).reshape(P, DB * 256)], 1)
    arrays["kc_nat"] = kc.reshape(DB, P, 256)
    arrays["vc_nat"] = vc.reshape(DB, P, 256)
    arrays["wkvT"] = f["state_wkv"][0].reshape(DB, KT, 2, HD, HD).transpose(2, 4, 1, 0, 3).reshape(P, 4096)
    arrays["shiftT"] = f["state_shift"][0].reshape(DB, KT, P).transpose(2, 1, 0).reshape(P, KT * DB)

    outs = {"y": (P, KT * T), "conv": (P, CT * 27), "kT": (64, NKV * (128 + TS)), "v_p": (P, 256), "v_s": (TS, 256),
            "p_ssm": (P, 1024), "s_ssm": (2, P, 4096), "shift": (P, KT * 9), "p_wkv": (P, 512), "s_wkv": (P, 4096),
            "s_kc": (DB, P - DL, 256), "s_vc": (DB, P - DL, 256)}
    nc = bacc.Bacc("TRN2", target_bir_lowering=False, num_devices=1)
    ins, given = {}, {}
    for n, w in arrays.items():
        given[f"in_{n}"] = np.ascontiguousarray(w)
        ins[n] = nc.dram_tensor(f"in_{n}", w.shape, F32, kind="ExternalInput").ap()
    drams = {n: nc.dram_tensor(f"out_{n}", sh, F32, kind="ExternalOutput").ap() for n, sh in outs.items()}
    decoder_trunk(nc, ins, drams)
    r = run(nc, [given], core_ids=[0])
    o = {n: np.asarray(r.results[0][f"out_{n}"]) for n in outs}

    y = o["y"].reshape(P, KT, T).transpose(2, 1, 0).reshape(T, D)
    conv = o["conv"].reshape(P, CT, 27).transpose(2, 1, 0).reshape(27, CONV)
    kT = o["kT"].reshape(HD, NKV, P + TS).transpose(2, 1, 0)
    p_ssm = o["p_ssm"].reshape(P, NH, HD).transpose(1, 2, 0)
    s_ssm = o["s_ssm"].reshape(2, P, DB, 8, HD).transpose(2, 0, 3, 4, 1).reshape(DB, NH, HD, P)
    p_wkv = o["p_wkv"].reshape(2, HD, KT, HD).transpose(2, 0, 3, 1).reshape(NH, HD, HD)
    s_wkv = o["s_wkv"].reshape(2, HD, KT, DB, HD).transpose(3, 2, 0, 4, 1).reshape(DB, NH, HD, HD)
    shift = o["shift"].reshape(P, KT, 9).transpose(2, 1, 0).reshape(9, D)
    s_k = np.concatenate([o["s_kc"].reshape(DB, P - DL, NKV, HD), kT[P:].reshape(DB, DL, NKV, HD)], 1)
    s_v = np.concatenate([o["s_vc"].reshape(DB, P - DL, NKV, HD), o["v_s"].reshape(DB, DL, NKV, HD)], 1)
    res = (y[:TP].reshape(1, TP, D), y[TP:].reshape(DB, DL, D), p_ssm[None, None], conv[None, None, 0:3],
           kT[None, None, 0:P], o["v_p"].reshape(1, 1, P, NKV, HD), p_wkv[None, None], shift[None, 0:1],
           s_ssm[None], conv[3:].reshape(1, DB, 3, CONV), s_k[None], s_v[None], s_wkv[None], shift[1:].reshape(1, DB, D))
    return tuple(np.ascontiguousarray(w) for w in res)
```
